# Optimizing a Trainium2 kernel written in Bass

```python
import jax
import jax.numpy as jnp
from jax import lax

D_MODEL = 1024
BATCH = 1
SEQ = 256
DEPTH = 1

HEAD_DIM = 64
NSA_HEADS = 8
NSA_KV_HEADS = 2
NSA_GROUP = NSA_HEADS // NSA_KV_HEADS
NSA_WIDTH = NSA_HEADS * HEAD_DIM
NSA_KV_WIDTH = NSA_KV_HEADS * HEAD_DIM
CMP_LEN = 32
CMP_STRIDE = 16
CMP_HIDDEN = 128
SEL_BLOCK = 64
TOP_N = 8
WINDOW = 512
Q_BLOCK = 128
FORCE_BONUS = 1000.0
RWKV_HEADS = 8
RWKV_HEAD_DIM = 64
RWKV_WIDTH = RWKV_HEADS * RWKV_HEAD_DIM
DECAY_RANK = 64
AAA_RANK = 64
GATE_RANK = 128
GN_EPS = 64e-5
MEM_TOKENS = 256
MEM_HEADS = 4
MEM_HEAD_DIM = 128
MEM_WIDTH = MEM_HEADS * MEM_HEAD_DIM
N_BRANCHES = 3
BRANCH_WIDTH = 512
N_EXPERTS = 32
TOP_K = 4
EXPERT_FF = 1024
SWIGLU_ALPHA = 1.702
SWIGLU_LIMIT = 7.0

ROPE_THETA = 10000.0
RMS_EPS = 1e-6

SHIFT_WIDTH = 3 * RWKV_WIDTH + DECAY_RANK + AAA_RANK + GATE_RANK
IN_SPLITS = (NSA_WIDTH, 6 * NSA_KV_WIDTH, 3 * NSA_HEADS, SHIFT_WIDTH, MEM_WIDTH, N_BRANCHES * D_MODEL)
IN_WIDTH = NSA_WIDTH + 6 * NSA_KV_WIDTH + 3 * NSA_HEADS + SHIFT_WIDTH + MEM_WIDTH + N_BRANCHES * D_MODEL
RWKV_SPLITS = (RWKV_WIDTH, RWKV_WIDTH, RWKV_WIDTH, DECAY_RANK, AAA_RANK, GATE_RANK)

kernel_name = "hybrid_nsa_rwkv7_memory_moe"

def _split(t, widths):
    out, start = [], 0
    for w in widths:
        out.append(t[..., start:start + w])
        start += w
    return out

def rmsnorm(x, g):
    xf = x.astype(jnp.float32)
    y = xf * lax.rsqrt(jnp.mean(xf * xf, axis=-1, keepdims=True) + RMS_EPS)
    return (y * g.astype(jnp.float32)).astype(x.dtype)

def rope_tables(pos, dim):
    inv = ROPE_THETA ** (-jnp.arange(0, dim, 2, dtype=jnp.float32) / dim)
    ang = pos.astype(jnp.float32)[:, None] * inv[None, :]
    ang = jnp.concatenate([ang, ang], axis=-1)
    return jnp.cos(ang), jnp.sin(ang)

def apply_rope(x, cos, sin):
    x1, x2 = jnp.split(x, 2, axis=-1)
    rot = jnp.concatenate([-x2, x1], axis=-1)
    return (x * cos + rot * sin).astype(x.dtype)

def masked_softmax(s, mask):
    s = jnp.where(mask, s.astype(jnp.float32), -jnp.inf)
    m = jnp.max(s, axis=-1, keepdims=True)
    m = jnp.where(jnp.isfinite(m), m, 0.0)
    e = jnp.where(mask, jnp.exp(s - m), 0.0)
    return e / jnp.maximum(jnp.sum(e, axis=-1, keepdims=True), 1e-30)

def nsa_mixer(q, kv, gate_logits, q_norm, k_norm, cmp_pe, cmp_w1, cmp_b1, cmp_w2, cos, sin):
    B, S, _ = q.shape
    G, HG, Dh = NSA_KV_HEADS, NSA_GROUP, HEAD_DIM
    scale = Dh ** -0.5
    pos = jnp.arange(S)
    q = apply_rope(rmsnorm(q.reshape(B, S, G, HG, Dh), q_norm), cos[:, None, None], sin[:, None, None])
    k_cmp, v_cmp, k_slc, v_slc, k_win, v_win = [t.reshape(B, S, G, Dh) for t in jnp.split(kv, 6, axis=-1)]

    n_cmp = (S - CMP_LEN) // CMP_STRIDE + 1
    cmp_start = jnp.arange(n_cmp) * CMP_STRIDE
    cmp_end = cmp_start + CMP_LEN - 1
    gather_idx = cmp_start[:, None] + jnp.arange(CMP_LEN)[None, :]

    def compress(t, j):
        blocks = t[:, gather_idx] + cmp_pe[j][None, None, :, None, :]
        blocks = jnp.moveaxis(blocks, 3, 2).reshape(B, n_cmp, G, CMP_LEN * Dh)
        return jax.nn.gelu(blocks @ cmp_w1[j] + cmp_b1[j]) @ cmp_w2[j]

    cc, sc = rope_tables(cmp_end, Dh)
    kc = apply_rope(rmsnorm(compress(k_cmp, 0), k_norm[0]), cc[:, None], sc[:, None])
    vc = compress(v_cmp, 1)
    s_cmp = jnp.einsum('bsghd,bcgd->bsghc', q, kc) * scale
    p_cmp = masked_softmax(s_cmp, (cmp_end[None, :] <= pos[:, None])[None, :, None, None, :])
    o_cmp = jnp.einsum('bsghc,bcgd->bsghd', p_cmp.astype(vc.dtype), vc)

    n_sel = S // SEL_BLOCK
    n_top = min(TOP_N, n_sel)
    blk = jnp.arange(n_sel)
    blk_start = blk * SEL_BLOCK
    cover = ((cmp_start[:, None] < blk_start[None, :] + SEL_BLOCK)
             & (cmp_start[:, None] + CMP_LEN > blk_start[None, :])).astype(jnp.float32)
    imp = jnp.einsum('bsghc,cn->bsgn', p_cmp, cover)
    cur = pos // SEL_BLOCK
    forced = (blk[None, :] == 0) | (blk[None, :] == cur[:, None]) | (blk[None, :] == cur[:, None] - 1)
    imp = jnp.where(forced[None, :, None, :], imp + FORCE_BONUS, imp)
    imp = jnp.where((blk[None, :] <= cur[:, None])[None, :, None, :], imp, -jnp.inf)
    _, sel_idx = lax.top_k(imp, n_top)

    ks = apply_rope(rmsnorm(k_slc, k_norm[1]), cos[:, None], sin[:, None])
    kw = apply_rope(rmsnorm(k_win, k_norm[2]), cos[:, None], sin[:, None])
    k_blocks = jnp.transpose(ks.reshape(B, n_sel, SEL_BLOCK, G, Dh), (0, 3, 1, 2, 4))
    v_blocks = jnp.transpose(v_slc.reshape(B, n_sel, SEL_BLOCK, G, Dh), (0, 3, 1, 2, 4))
    kw_pad = jnp.concatenate([jnp.zeros((B, WINDOW, G, Dh), kw.dtype), kw], axis=1)
    vw_pad = jnp.concatenate([jnp.zeros((B, WINDOW, G, Dh), v_win.dtype), v_win], axis=1)
    n_chunks = S // Q_BLOCK
    b_ix = jnp.arange(B)[:, None, None, None]
    g_ix = jnp.arange(G)[None, None, :, None]

    def to_chunks(t):
        return jnp.moveaxis(t.reshape((B, n_chunks, Q_BLOCK) + t.shape[2:]), 1, 0)

    def from_chunks(t):
        return jnp.moveaxis(t, 0, 1).reshape((B, S) + t.shape[3:])

    def chunk_fn(args):
        c, qc, idx = args
        tq = c * Q_BLOCK + jnp.arange(Q_BLOCK)
        k_sel = k_blocks[b_ix, g_ix, idx]
        v_sel = v_blocks[b_ix, g_ix, idx]
        s = jnp.einsum('bqghd,bqgnld->bqghnl', qc, k_sel) * scale
        kpos = idx[..., None] * SEL_BLOCK + jnp.arange(SEL_BLOCK)
        m = (kpos <= tq[None, :, None, None, None]).reshape(B, Q_BLOCK, G, 1, n_top * SEL_BLOCK)
        p = masked_softmax(s.reshape(B, Q_BLOCK, G, HG, n_top * SEL_BLOCK), m)
        p = p.reshape(B, Q_BLOCK, G, HG, n_top, SEL_BLOCK)
        o_s = jnp.einsum('bqghnl,bqgnld->bqghd', p.astype(v_sel.dtype), v_sel)
        kb = lax.dynamic_slice_in_dim(kw_pad, c * Q_BLOCK, WINDOW + Q_BLOCK, axis=1)
        vb = lax.dynamic_slice_in_dim(vw_pad, c * Q_BLOCK, WINDOW + Q_BLOCK, axis=1)
        kp = c * Q_BLOCK - WINDOW + jnp.arange(WINDOW + Q_BLOCK)
        mw = (kp[None, :] >= 0) & (kp[None, :] <= tq[:, None]) & (kp[None, :] > tq[:, None] - WINDOW)
        sw = jnp.einsum('bqghd,bkgd->bqghk', qc, kb) * scale
        pw = masked_softmax(sw, mw[None, :, None, None, :])
        o_w = jnp.einsum('bqghk,bkgd->bqghd', pw.astype(vb.dtype), vb)
        return o_s, o_w

    o_slc, o_win = lax.map(chunk_fn, (jnp.arange(n_chunks), to_chunks(q), to_chunks(sel_idx)))
    o_slc, o_win = from_chunks(o_slc), from_chunks(o_win)

    gates = jax.nn.sigmoid(gate_logits.astype(jnp.float32)).reshape(B, S, G, HG, 3).astype(q.dtype)
    o = gates[..., 0:1] * o_cmp + gates[..., 1:2] * o_slc + gates[..., 2:3] * o_win
    return o.reshape(B, S, NSA_WIDTH)

def rwkv7_mixer(p, shift_mix, w0, w_up, a0, a_up, g_up, k_k, k_a, r_k, ln_w, ln_b):
    B, S, _ = p.shape
    H, N = RWKV_HEADS, RWKV_HEAD_DIM
    prev = jnp.concatenate([jnp.zeros_like(p[:, :1]), p[:, :-1]], axis=1)
    p = p + (prev - p) * shift_mix
    r, k, v, xw, xa, xg = _split(p, RWKV_SPLITS)
    w = -jax.nn.softplus(-(w0 + jnp.tanh(xw) @ w_up)) - 0.5
    a = jax.nn.sigmoid(a0 + xa @ a_up)
    g = jax.nn.sigmoid(xg) @ g_up

    def heads(t):
        return t.reshape(B, S, H, N).astype(jnp.float32)

    kk = heads(k * k_k)
    kk = kk / jnp.maximum(jnp.linalg.norm(kk, axis=-1, keepdims=True), 1e-12)
    k = k * (1.0 + (a - 1.0) * k_a)
    r4, k4, v4, a4 = heads(r), heads(k), heads(v), heads(a)
    decay = jnp.exp(-jnp.exp(heads(w)))

    def step(state, inp):
        r_t, w_t, k_t, v_t, a_t, b_t = inp
        sa = jnp.einsum('bhvk,bhk->bhv', state, a_t)
        state = (state * w_t[:, :, None, :] + sa[..., None] * b_t[:, :, None, :]
                 + v_t[..., None] * k_t[:, :, None, :])
        return state, jnp.einsum('bhvk,bhk->bhv', state, r_t)

    seqs = tuple(jnp.moveaxis(t, 1, 0) for t in (r4, decay, k4, v4, -kk, kk * a4))
    _, y = lax.scan(step, jnp.zeros((B, H, N, N), jnp.float32), seqs)
    y = jnp.moveaxis(y, 0, 1)
    mu = jnp.mean(y, axis=-1, keepdims=True)
    var = jnp.mean(jnp.square(y - mu), axis=-1, keepdims=True)
    y = ((y - mu) * lax.rsqrt(var + GN_EPS)).reshape(B, S, H * N) * ln_w + ln_b
    bonus = jnp.sum(r4 * k4 * r_k, axis=-1, keepdims=True) * v4
    y = (y + bonus.reshape(B, S, H * N)) * g
    return y.astype(p.dtype)

def memory_mixer(q, mem_n, w_kv, q_norm, k_norm):
    B, S, _ = q.shape
    M = mem_n.shape[1]
    q = rmsnorm(q.reshape(B, S, MEM_HEADS, MEM_HEAD_DIM), q_norm)
    k, v = jnp.split(mem_n @ w_kv, 2, axis=-1)
    k = rmsnorm(k.reshape(B, M, MEM_HEADS, MEM_HEAD_DIM), k_norm)
    v = v.reshape(B, M, MEM_HEADS, MEM_HEAD_DIM)
    s = jnp.einsum('bshd,bmhd->bhsm', q, k) * (MEM_HEAD_DIM ** -0.5)
    pr = jax.nn.softmax(s.astype(jnp.float32), axis=-1)
    o = jnp.einsum('bhsm,bmhd->bshd', pr.astype(v.dtype), v)
    return o.reshape(B, S, MEM_WIDTH)

def moe_ffn(h, router_w, router_b, w1, b1, w2, b2):
    B, S, D = h.shape
    t = h.reshape(B * S, D)
    logits = (t @ router_w + router_b).astype(jnp.float32)
    top_v, top_i = lax.top_k(logits, TOP_K)
    top_w = jax.nn.softmax(top_v, axis=-1)
    gate = jnp.sum(jax.nn.one_hot(top_i, N_EXPERTS, dtype=jnp.float32) * top_w[..., None], axis=1)
    gate = gate.astype(t.dtype)
    out = jnp.zeros_like(t)
    for e in range(N_EXPERTS):
        hid = t @ w1[e] + b1[e]
        x_glu = jnp.minimum(hid[:, ::2], SWIGLU_LIMIT)
        x_lin = jnp.clip(hid[:, 1::2], -SWIGLU_LIMIT, SWIGLU_LIMIT)
        act = x_glu * jax.nn.sigmoid(SWIGLU_ALPHA * x_glu) * (x_lin + 1.0)
        out = out + gate[:, e:e + 1] * (act @ w2[e] + b2[e])
    return out.reshape(B, S, D)

def setup_inputs(seed: int = 0) -> dict:
    key = jax.random.key(seed)
    ks = iter(jax.random.split(key, 48))
    L = DEPTH

    def nrm(shape, scale):
        return scale * jax.random.normal(next(ks), shape, jnp.float32)

    def gain(shape):
        return 1.0 + 0.05 * jax.random.normal(next(ks), shape, jnp.float32)

    return {
        "x": nrm((BATCH, SEQ, D_MODEL), 1.0),
        "mem": nrm((BATCH, MEM_TOKENS, D_MODEL), 1.0),
        "g_mix": gain((L, D_MODEL)),
        "g_mem": gain((L, D_MODEL)),
        "w_in": nrm((L, D_MODEL, IN_WIDTH), D_MODEL ** -0.5),
        "b_merge": nrm((L, N_BRANCHES * D_MODEL), 0.01),
        "nsa_q_norm": gain((L, HEAD_DIM)),
        "nsa_k_norm": gain((L, 3, HEAD_DIM)),
        "cmp_pe": nrm((L, 2, CMP_LEN, HEAD_DIM), 0.1),
        "cmp_w1": nrm((L, 2, CMP_LEN * HEAD_DIM, CMP_HIDDEN), (CMP_LEN * HEAD_DIM) ** -0.5),
        "cmp_b1": nrm((L, 2, CMP_HIDDEN), 0.01),
        "cmp_w2": nrm((L, 2, CMP_HIDDEN, HEAD_DIM), CMP_HIDDEN ** -0.5),
        "rwkv_shift_mix": jax.random.uniform(next(ks), (L, SHIFT_WIDTH), jnp.float32),
        "rwkv_w0": -1.0 + nrm((L, RWKV_WIDTH), 0.5),
        "rwkv_w_up": nrm((L, DECAY_RANK, RWKV_WIDTH), 0.1),
        "rwkv_a0": nrm((L, RWKV_WIDTH), 0.1),
        "rwkv_a_up": nrm((L, AAA_RANK, RWKV_WIDTH), 0.1),
        "rwkv_g_up": nrm((L, GATE_RANK, RWKV_WIDTH), GATE_RANK ** -0.5),
        "rwkv_k_k": 0.85 + nrm((L, RWKV_WIDTH), 0.05),
        "rwkv_k_a": 1.0 + nrm((L, RWKV_WIDTH), 0.05),
        "rwkv_r_k": nrm((L, RWKV_HEADS, RWKV_HEAD_DIM), 0.1),
        "rwkv_ln_w": gain((L, RWKV_WIDTH)),
        "rwkv_ln_b": nrm((L, RWKV_WIDTH), 0.01),
        "mem_w_kv": nrm((L, D_MODEL, 2 * MEM_WIDTH), D_MODEL ** -0.5),
        "mem_q_norm": gain((L, MEM_HEAD_DIM)),
        "mem_k_norm": gain((L, MEM_HEAD_DIM)),
        "w_branch": nrm((L, N_BRANCHES, BRANCH_WIDTH, D_MODEL), BRANCH_WIDTH ** -0.5),
        "w_out": nrm((L, D_MODEL, D_MODEL), D_MODEL ** -0.5),
        "g_ffn": gain((L, D_MODEL)),
        "router_w": nrm((L, D_MODEL, N_EXPERTS), D_MODEL ** -0.5),
        "router_b": nrm((L, N_EXPERTS), 0.01),
        "exp_w1": nrm((L, N_EXPERTS, D_MODEL, 2 * EXPERT_FF), D_MODEL ** -0.5),
        "exp_b1": nrm((L, N_EXPERTS, 2 * EXPERT_FF), 0.01),
        "exp_w2": nrm((L, N_EXPERTS, EXPERT_FF, D_MODEL), EXPERT_FF ** -0.5),
        "exp_b2": nrm((L, N_EXPERTS, D_MODEL), 0.01),
    }

def reference(x, mem, g_mix, g_mem, w_in, b_merge, nsa_q_norm, nsa_k_norm, cmp_pe, cmp_w1, cmp_b1, cmp_w2,
              rwkv_shift_mix, rwkv_w0, rwkv_w_up, rwkv_a0, rwkv_a_up, rwkv_g_up, rwkv_k_k, rwkv_k_a, rwkv_r_k,
              rwkv_ln_w, rwkv_ln_b, mem_w_kv, mem_q_norm, mem_k_norm, w_branch, w_out, g_ffn,
              router_w, router_b, exp_w1, exp_b1, exp_w2, exp_b2):
    B, S, D = x.shape
    cos, sin = rope_tables(jnp.arange(S), HEAD_DIM)
    for l in range(DEPTH):
        h = rmsnorm(x, g_mix[l])
        q_nsa, kv_nsa, gate_nsa, p_rwkv, q_mem, merge_logits = _split(h @ w_in[l], IN_SPLITS)
        o_a = nsa_mixer(q_nsa, kv_nsa, gate_nsa, nsa_q_norm[l], nsa_k_norm[l], cmp_pe[l], cmp_w1[l],
                        cmp_b1[l], cmp_w2[l], cos, sin)
        o_b = rwkv7_mixer(p_rwkv, rwkv_shift_mix[l], rwkv_w0[l], rwkv_w_up[l], rwkv_a0[l], rwkv_a_up[l],
                          rwkv_g_up[l], rwkv_k_k[l], rwkv_k_a[l], rwkv_r_k[l], rwkv_ln_w[l], rwkv_ln_b[l])
        o_m = memory_mixer(q_mem, rmsnorm(mem, g_mem[l]), mem_w_kv[l], mem_q_norm[l], mem_k_norm[l])
        branches = jnp.einsum('nbsc,ncd->bsnd', jnp.stack([o_a, o_b, o_m], axis=0), w_branch[l])
        gates = jax.nn.sigmoid((merge_logits + b_merge[l]).astype(jnp.float32)).reshape(B, S, N_BRANCHES, D)
        mixed = jnp.sum(gates.astype(branches.dtype) * branches, axis=2)
        x = x + mixed @ w_out[l]
        x = x + moe_ffn(rmsnorm(x, g_ffn[l]), router_w[l], router_b[l], exp_w1[l], exp_b1[l],
                        exp_w2[l], exp_b2[l])
    return x


_drawn_inputs = setup_inputs


def setup_inputs(seed=0):
    import zlib

    import numpy as np

    out = dict(_drawn_inputs(seed))
    spreads = {}
    factors = {'g_mem': 3.305,
     'b_merge': 8.0,
     'nsa_q_norm': 3.03,
     'nsa_k_norm': 3.78,
     'cmp_b1': 24.222,
     'rwkv_k_k': 175.593,
     'rwkv_ln_b': 13.524,
     'mem_q_norm': 8.0,
     'mem_k_norm': 8.0,
     'exp_b1': 21.756,
     'exp_b2': 22.525,
     'rwkv_a0': 3.815,
     'rwkv_k_a': 3.308,
     'rwkv_ln_w': 3.945,
     'router_b': 3.385,
     'cmp_pe': 2.806}
    for name, (base, spread) in spreads.items():
        noise = np.random.default_rng([zlib.crc32(name.encode()), seed]).standard_normal(out[name].shape)
        drawn = base * np.exp(spread * noise) if base else spread * noise
        out[name] = jnp.asarray(drawn.astype(out[name].dtype))
    for name, factor in factors.items():
        out[name] = (out[name] * factor).astype(out[name].dtype)
    return out
```

```python
from contextlib import ExitStack

import numpy as np

import concourse.bass as bass
from concourse import mybir

ALU = mybir.AluOpType
ACT = mybir.ActivationFunctionType
AX = mybir.AxisListType
F32 = mybir.dt.float32
U32 = mybir.dt.uint32
I32 = mybir.dt.int32

P = 128
D = 1024
S = 256
TT = S // P
KD = D // P
DH = 64
NH = 8
NG = 2
CMP_L, CMP_ST = 32, 16
NC = (S - CMP_L) // CMP_ST + 1
CH = 64
NCH = S // CH
MH, MD = 4, 128
NE, TOPK, FF = 32, 4, 1024
CAP = 64
ROUNDS = -(-S // CAP)
NEG = -1.0e30
EPS = 1e-6
GN_EPS = 64e-5
EM05 = float(np.exp(-0.5))
UNIT = 4096
N1, N2 = 3, 6

VEC = {}
for _name, _n in (("g_mix", 8), ("g_mem", 8), ("g_ffn", 8), ("b_merge", 24), ("mix", 14), ("w0", 4), ("a0", 4),
                  ("k_k", 4), ("k_a", 4), ("r_k", 4), ("ln_w", 4), ("ln_b", 4), ("cmp_b1", 2),
                  ("mq_n", 1), ("mk_n", 1)):
    VEC[_name] = (sum(n for _, n in VEC.values()), _n)
NVEC = sum(n for _, n in VEC.values())

CONST = {}
for _name, _n in (("ident", P), ("low", P), ("upp", P), ("uppi", P), ("heads", P), ("before", P), ("ones", P),
                  ("up1", P), ("up2", P), ("up4", P), ("up8", P), ("up16", P), ("up32", P),
                  ("lo1", P), ("lo2", P), ("lo4", P), ("lo8", P), ("lo16", P),
                  ("causal", 2 * P), ("cmpneg", 2 * NC), ("cmpok", 2 * NC), ("cos", 2 * DH), ("sin", 2 * DH),
                  ("twice", CAP), ("ccos", DH), ("csin", DH), ("slots", CAP), ("experts", NE), ("half", 32), ("gn_eps", 1)):
    CONST[_name] = (sum(n for _, n in CONST.values()), _n)
NCONST = sum(n for _, n in CONST.values())


def shape_constants():
    c = np.zeros((P, NCONST), np.float32)

    def put(name, a):
        o, n = CONST[name]
        c[:a.shape[0], o:o + n] = a.reshape(a.shape[0], n)

    i, j = np.arange(P)[:, None], np.arange(P)[None, :]
    chunk = i // CH == j // CH
    put("ident", (i == j) * 1.0)
    put("low", (i > j) * chunk * 1.0)
    put("upp", (i < j) * chunk * 1.0)
    put("uppi", (i <= j) * chunk * 1.0)
    put("heads", (i // DH == j // DH) * 1.0)
    put("before", (i < j) * 1.0)
    put("ones", np.ones((P, P)))
    for n in (1, 2, 4, 8, 16, 32):
        off = (i // (2 * n) == j // (2 * n)) & (i // n % 2 == 0) & (j // n % 2 == 1)
        put(f"up{n}", off * 1.0)
        if n < 32:
            put(f"lo{n}", off.T * 1.0)
    put("causal", np.concatenate([np.zeros((P, P)), np.where(j <= i, 0.0, NEG)], 1))
    pos = np.arange(P)[:, None, None] + P * np.arange(TT)[None, :, None]
    end = np.arange(NC)[None, None, :] * CMP_ST + CMP_L - 1
    put("cmpneg", np.where(end <= pos, 0.0, NEG))
    put("cmpok", (end <= pos) * 1.0)
    inv = np.float32(10000.0) ** (-np.arange(0, DH, 2, dtype=np.float32) / np.float32(DH))

    def rope(at):
        ang = at.astype(np.float32)[..., None] * inv
        cos, sin = np.cos(ang), np.sin(ang)
        return np.concatenate([cos, cos], -1), np.concatenate([-sin, sin], -1)

    cos, sin = rope(pos[..., 0])
    put("cos", cos)
    put("twice", (i[:, 0:1] % CAP == np.arange(CAP)) * 1.0)
    put("sin", sin)
    cos, sin = rope(np.arange(NC) * CMP_ST + CMP_L - 1)
    put("ccos", cos)
    put("csin", sin)
    put("slots", np.tile(np.arange(CAP), (P, 1)))
    put("experts", np.tile(np.arange(NE), (P, 1)))
    put("gn_eps", np.full((P, 1), GN_EPS))
    put("half", np.full((P, 32), -0.5))
    return c


UNITS = ([("cmp", g, t, 4, 0) for t in range(TT) for g in range(NG)]
         + [(kind, g * 4 + h, t, 4 if t == 0 else 2, t + 1) for kind in ("slc", "win") for g in range(NG)
            for t in range(TT) for h in ((0,) if t == 0 else (0, 2))]
         + [("mem", h, t, 2, 2) for t in range(TT) for h in (0, 2)])
LEVELS = (2, 4, 8, 16, 32)
SHIFT_UNITS = ((0, 4), (4, 4), (8, 4), (12, 2))
MERGE_T = 3 * KD


def attention_jobs():
    jobs = [("scores", 0), ("scores", 1)]
    for u in range(len(UNITS)):
        jobs += [("turn", u)] + ([("scores", u + 2)] if u + 2 < len(UNITS) else []) + [("values", u)]
    return jobs


def inverse_jobs():
    jobs = []
    for n in LEVELS:
        jobs += [("X", n, b) for b in range(4)]
        for b in range(4):
            jobs += [("MX", n, b)] + ([("XT", n, b)] if n < 32 else [])
    return jobs


JOBS = ([("hT", q, t) for t in range(TT) for q in range(2)] + [("mT", q, t) for t in range(TT) for q in range(2)]
        + [("shift", ct) for ct in range(0, 14, 2)]
        + [(w, t) for w in ("q", "kc", "vg", "qm", "km", "vm") for t in range(TT)]
        + [("kcT",), ("hid",), ("cmp2",), ("cT",)]
        + [("qkT", t, q) for t in range(TT) for q in range(3)]
        + [("memT", w, t) for w in "qk" for t in range(TT)]
        + attention_jobs()
        + [("oaT", t) for t in range(TT)] + [("omT", t) for t in range(TT)]
        + [("up", w, q) for w in "wag" for q in range(2)]
        + [("ksum", q) for q in range(2)] + [("bonus", q) for q in range(2)]
        + [("vtok", t) for t in range(TT)]
        + [("tok", w, t) for w in "akb" for t in range(TT)]
        + [("A", b) for b in range(4)] + [("B", b) for b in range(4)]
        + [(w, b) for w in ("Kk", "Rb", "Rk") for b in range(4)]
        + [("KV", t) for t in range(TT)]
        + inverse_jobs()
        + [("UW", b) for b in range(4)] + [("rhat", b) for b in range(4)]
        + [("Q", 0), ("Q", 1), ("PT", 1), ("Q", 2), ("PT", 2), ("state", 1), ("state", 2)]
        + [("Y", t) for t in range(TT)]
        + [("mean", q) for q in range(2)] + [("var", q) for q in range(2)]
        + [("merge", ct) for ct in range(0, MERGE_T, 2)]
        + [("branch", n, ct) for n in range(3) for ct in range(0, KD, 2)]
        + [("out", t, q) for t in range(TT) for q in range(2)]
        + [("h2T", q, t) for t in range(TT) for q in range(2)]
        + [("logits",), ("rank",), ("gateT",)])
NB = 8
BANK = {job: (n % NB, n // NB) for n, job in enumerate(JOBS)}
LAST_USE = [max(BANK[j][1] for j in JOBS if BANK[j][0] == b) + 1 for b in range(NB)]

W1_UNITS = (["shift0", "shift1", "shift2", "shift3", "q", "kc", "vg", "qm", "km", "vm", "cmp1"]
            + [f"merge{n}" for n in range(6)] + ["branch0", "branch1", "branch2", "out0", "out1"])
W1_AT = {name: n for n, name in enumerate(W1_UNITS)}

SEMS = """x_in const_in small_in late_in x_out
 v_step a_step g_step xsq_done xr_done xn_done pp_done wa_done xg_done
 qk_sq qk_ss qk_r qk_rot R_zero R_done ge_in tanh_in tanh_out ge_done kc_sq kc_r kc_rot
 qm_sq qm_r qm_n gate_raw m_ready e_ready cmp_ok values_done
 decay_done k_sq rk_done tilde_done MT_init lg_ss lg_exp
 state_done y_sq ob_done mix_done x1_sq x1_r xn2_done sel_done gat_done scratch_free x1_done
 P_ready pg_ready g_full xg_ready h_full h_out t_full t_out x_ready t_ready a_ready o_half o_full o_free v2_step
 y_full y_out""".split()


class Arena:

    def __init__(self, tensor, size):
        self.tensor, self.size, self.at = tensor, size, 0

    def take(self, *dims, parts=P):
        n = int(np.prod(dims))
        assert self.at + n <= self.size, (self.at, n)
        v = self.tensor[0:parts, self.at:self.at + n]
        self.at += n
        if len(dims) == 2:
            v = v.rearrange("p (a b) -> p a b", a=dims[0])
        elif len(dims) == 3:
            v = v.rearrange("p (a b c) -> p a b c", a=dims[0], b=dims[1])
        elif len(dims) == 4:
            v = v.rearrange("p (a b c d) -> p a b c d", a=dims[0], b=dims[1], c=dims[2])
        return v


class Steps:

    def __init__(self, eng, own, bank_free, bank_full):
        self.eng, self.own, self.bank_free, self.bank_full = eng, own, bank_free, bank_full
        self.counts, self.last = {}, None

    def do(self, ins, sem=None):
        sem = sem or self.own
        self.counts[sem.name] = self.counts.get(sem.name, 0) + 1
        ins.then_inc(sem, 1)
        self.last = (sem, self.counts[sem.name])

    def free(self, ins, job):
        b, used = BANK[job]
        ins.then_inc(self.bank_free[b], 1)
        self.last = (self.bank_free[b], used + 1)

    def full(self, job):
        b, used = BANK[job]
        self.eng.wait_ge(self.bank_full[b], used + 1)

    def settle(self):
        self.eng.wait_ge(*self.last)


def bc(ap, axis, n):
    v = ap.unsqueeze(axis)
    shape = list(v.shape)
    shape[axis] = n
    return v.to_broadcast(shape)


def build(nc, ins, out):
    with ExitStack() as ctx:
        arena_size = (nc.sbuf_bytes_remaining - 256) // 4
        arena = Arena(ctx.enter_context(nc.sbuf_tensor("arena", [P, arena_size], F32)), arena_size)
        psum = ctx.enter_context(nc.psum_tensor("banks", [P, NB, 512], F32))
        s = {n: ctx.enter_context(nc.semaphore(n)) for n in SEMS}
        bank_full = [ctx.enter_context(nc.semaphore(f"bank_full{b}")) for b in range(NB)]
        bank_free = [ctx.enter_context(nc.semaphore(f"bank_free{b}")) for b in range(NB)]
        w1_in = [ctx.enter_context(nc.semaphore(f"weights_in{b}")) for b in range(N1)]
        moe_in = [ctx.enter_context(nc.semaphore(f"moe_in{b}")) for b in range(N2)]
        A = arena
        slots = [A.take(UNIT) for _ in range(N1)]
        const = A.take(NCONST)
        vec = A.take(NVEC)

        def C(name, *dims, parts=P):
            o, n = CONST[name]
            v = const[0:parts, o:o + n]
            return v.rearrange("p (a b) -> p a b", a=dims[0]) if dims else v

        def V(name, i=None):
            o, n = VEC[name]
            return vec[:, o:o + n] if i is None else vec[:, o + i:o + i + 1]

        ident = C("ident")
        hw0, ha0, hbm, omka = A.take(4), A.take(4), A.take(24), A.take(4)
        router_w = A.take(KD, NE)
        router_b = A.take(NE)
        b2_sb = A.take(D)
        stat = A.take(8)
        rstd = A.take(8)
        moe_base = A.at
        up_w, up_g = A.take(512), A.take(512)
        hT = A.take(KD, S)
        oaT, omT, obT = A.take(4, S), A.take(4, S), A.take(4, S)
        region = A.at

        xs, ms = A.take(TT, D), A.take(TT, D)
        mT = A.take(KD, S)
        pbuf = A.take(14, S + 1)
        qk = A.take(TT, 12, DH)
        kcv = A.take(TT, 2, P)
        vg = A.take(TT, 280)
        qm, km, vm = A.take(TT, MH, MD), A.take(TT, MH, MD), A.take(TT, MH, MD)
        qkT = A.take(12, S, parts=DH)
        R = A.take(2, 16, 31)
        qmT, kmT = A.take(MH, S), A.take(MH, S)
        cw2, pe_sb = A.take(2, DH), A.take(2, 16)
        nwt = A.take(12, DH)
        kn0 = A.take(DH, parts=NC)
        rs, rr = A.take(24), A.take(24)
        rsm, rrm = A.take(16), A.take(16)
        gates = A.take(TT, NH * 3)
        hbias, hx, hu, ge = A.take(2), A.take(2, 30), A.take(2, 30), A.take(2, 30)
        ctok, csq, crot = A.take(2, 2, DH, parts=NC), A.take(2, DH, parts=NC), A.take(2, DH, parts=NC)
        cs2, cr2 = A.take(2, parts=NC), A.take(2, parts=NC)
        kcT = A.take(2, NC, parts=DH)
        osum, omem = A.take(TT, NH, DH), A.take(TT, MH, MD)
        shared = A.at
        rot1, rot2 = A.take(TT, 12, DH), A.take(TT, 12, DH)
        sqx = rot1.rearrange("p a b c -> p (a b c)")[:, 0:D]
        A.at = shared
        sb_s, sb_e, sb_eT = A.take(2, 512), A.take(2, 512), A.take(2, 512)
        mx, nmx, sm, fac = A.take(2, 4), A.take(2, 4), A.take(2, 4), A.take(2, 4)
        otmp = A.take(2, 256)

        A.at = region
        pp = A.take(14, S)
        A.at = region
        Rb, Rk = A.take(16, P), A.take(16, P)
        til = {w: A.take(NH, S, parts=DH) for w in "abkr"}
        gg, bon = A.take(4, S), A.take(4, S)
        DC = A.take(NH, NCH, parts=DH)
        tok = {w: A.take(TT, NH, DH) for w in "vkb"}
        KA = A.take(16, P)
        scratch = A.at
        dE, Dc = A.take(16, CH + 1), A.take(16, CH + 1)
        Di, aa, kkn, tmp = A.take(4, S), A.take(4, S), A.take(4, S), A.take(4, S)
        A.at = scratch
        Mm = A.take(16, P)
        Am, Tm = A.take(16, P), A.take(16, P)
        Xm = A.take(4, 512)
        UW = A.take(16, P)
        Kk = UW
        pat = UW.rearrange("p a b -> p (a b)")[:, 0:16 * (CH + 1)]
        A.at = scratch
        yb = A.take(4, S)
        yq = A.take(4, S)
        PT, Qs = A.take(3, NH, DH, parts=DH), A.take(3, NH, DH, parts=DH)
        assert A.at <= scratch + 6144
        A.at = scratch + 6144
        Ss = A.take(3, NH, DH, parts=DH)
        stmp = A.take(NH, DH, parts=DH)

        A.at = region
        x1 = A.take(TT, D)
        xn2 = A.take(TT, D)
        rankR, gateR = A.take(TT, ROUNDS * NE + 2), A.take(TT, ROUNDS * NE + 2)
        b1_sb = A.take(NE, 16)
        Pk, PG = A.take(TT, 2, CAP), A.take(TT, 2, CAP)
        xg, act = A.take(KD, 2 * CAP), A.take(KD, CAP)
        hraw = A.take(2, 512)
        hb, xlo, xhi, th = A.take(2, 4 * CAP), A.take(2, 2 * CAP), A.take(2, 2 * CAP), A.take(2, 2 * CAP)
        osb = A.take(D)
        pgt = A.take(2, S)
        nrounds = A.take(1).bitcast(I32)
        nz = A.take(2)
        mixT = A.take(KD, S)
        moe_top = arena_size - 3 * UNIT
        assert A.at <= moe_top, (A.at, moe_top)
        h2T = A.take(KD, S)
        lg, sel, gat = A.take(TT, NE), A.take(TT, NE), A.take(TT, NE)
        top, idx, idf = A.take(TT, 8), A.take(TT, 8).bitcast(U32), A.take(TT, 8)
        et, es, er = A.take(TT, 4), A.take(TT), A.take(TT)
        rk1, cnt = A.take(TT, NE), A.take(NE)
        cm = A.take(8)
        gT = hT.rearrange("p k s -> p (k s)")[:, 0:S]
        msum = A.take(2, S)
        mprod = A.take(2, 2 * S)
        tg = A.take(MERGE_T, S)
        slots2 = slots + [arena.tensor[:, moe_top + i * UNIT:moe_top + (i + 1) * UNIT] for i in range(3)]

        def B(job, parts=P):
            return psum[0:parts, BANK[job][0], :]

        def taken(eng, job):
            b, used = BANK[job]
            eng.wait_ge(bank_free[b], used + 1)

        def filled(eng, job):
            b, used = BANK[job]
            eng.wait_ge(bank_full[b], used + 1)

        def load_rounds(eng):
            eng.wait_ge(s["scratch_free"], 1)
            return eng.value_load(nrounds[0:1, 0:1], min_val=1, max_val=ROUNDS)

        block = ctx.enter_context(nc.Block())

        @block.sync
        def _(sp):
            rows = "b (t p) d -> p (b t) d"
            sp.dma_start(xs, ins["x"].rearrange(rows, p=P)).then_inc(s["x_in"], 16)
            sp.dma_start(ms, ins["mem"].rearrange(rows, p=P)).then_inc(s["x_in"], 16)
            sp.dma_start(const, ins["const"]).then_inc(s["const_in"], 16)
            sp.dma_start(vec, ins["vec"]).then_inc(s["const_in"], 16)
            last = {"shift0": ("shift", 2), "shift1": ("shift", 6), "shift2": ("shift", 10), "shift3": ("shift", 12),
                    "cmp1": ("hid",), "branch0": ("branch", 0, 6), "branch1": ("branch", 1, 6),
                    "branch2": ("branch", 2, 6), "out0": ("out", 1, 1), "out1": ("out", 1, 1)}
            last |= {w: (w, 1) for w in ("q", "kc", "vg", "qm", "km", "vm")}
            last |= {f"merge{n}": ("merge", 4 * n + 2) for n in range(6)}
            for n, name in enumerate(W1_UNITS):
                if n >= N1:
                    filled(sp, last[W1_UNITS[n - N1]])
                sp.dma_start(slots[n % N1], ins["weights"][n]).then_inc(w1_in[n % N1], 16)
                if n == N1 - 1:
                    for dst, src in ((up_w, ins["up"][:, 0:512]), (up_g, ins["up"][:, 512:1024]),
                                     (cw2.rearrange("p a b -> p (a b)"), ins["cmp_w2"]),
                                     (nwt.rearrange("p a b -> p (a b)"), ins["head_norms"].partition_broadcast(P)),
                                     (kn0, ins["cmp_norm"].partition_broadcast(NC)),
                                     (pe_sb.rearrange("p a b -> p (a b)"), ins["cmp_pe"]),
                                     (router_w.rearrange("p a b -> p (a b)"), ins["router_w"]),
                                     (router_b[0:1], ins["router_b"]), (b2_sb[0:NE], ins["exp_b2"])):
                        sp.dma_start(dst, src).then_inc(s["small_in"], 16)
                if name == "merge0":
                    filled(sp, ("Y", 1))
                    sp.dma_start(x1, ins["x"].rearrange(rows, p=P)).then_inc(s["late_in"], 16)
                    sp.dma_start(b1_sb.rearrange("p a b -> p (a b)"), ins["exp_b1"]).then_inc(s["late_in"], 16)
            filled(sp, last["out1"])
            sp.sem_inc(s["h_full"], 4)
            sp.sem_inc(s["o_half"], 1)
            sp.sem_inc(s["o_full"], 1)
            rounds = load_rounds(sp)
            with sp.Fori(0, rounds) as r:
                with sp.Fori(0, NE) as e:
                    for j in range(N2):
                        if j < 4:
                            sp.wait_ge(s["h_full"], (r * NE + e) * 4 + (j + 1))
                        else:
                            sp.wait_ge(s["o_half"] if j == 4 else s["o_full"], r * NE + e + 1)
                        sp.dma_start(slots2[j], ins["experts"][bass.ds(e, 1), j].rearrange("e p n -> (e p) n")
                                     ).then_inc(moe_in[j], 16)
            sp.wait_ge(s["y_out"], TT)
            sp.dma_start(out.rearrange(rows, p=P), x1).then_inc(s["x_out"], 16)
            sp.wait_ge(s["x_out"], 16)

        @block.gpsimd
        def _(eng):
            def inv_sqrt(after, n, dst, src, width, sem, parts=P):
                eng.wait_ge(after, n)
                eng.tensor_tensor(dst, src, C("half", parts=parts)[:, 0:width], ALU.pow).then_inc(sem, 1)

            eng.memset(pbuf[:, :, 0:1], 0.0).then_inc(s["R_zero"], 1)
            eng.wait_ge(s["const_in"], 32)
            inv_sqrt(s["xsq_done"], 1, rstd[:, 0:4], stat[:, 0:4], 4, s["xr_done"])
            taken(eng, ("q", 1))
            taken(eng, ("kc", 1))
            eng.tensor_tensor(rot1, qk, qk, ALU.mult).then_inc(s["qk_sq"], 1)
            inv_sqrt(s["qk_ss"], 1, rr, rs, 24, s["qk_r"])
            inv_sqrt(s["qm_sq"], 1, rrm, rsm, 16, s["qm_r"])
            inv_sqrt(s["kc_sq"], 1, cr2, cs2, 2, s["kc_r"], NC)
            inv_sqrt(s["x1_sq"], 1, rstd[:, 4:6], stat[:, 4:6], 2, s["x1_r"])

        @block.vector
        def _(eng):
            v = Steps(eng, s["v_step"], bank_free, bank_full)
            do, free, full, settle = v.do, v.free, v.full, v.settle
            tt, ts, stt, cp = eng.tensor_tensor, eng.tensor_scalar, eng.scalar_tensor_tensor, eng.tensor_copy

            def row_max(dst, src):
                return eng.tensor_reduce(dst, src, AX.X, ALU.max)

            def row_sum(dst, src):
                return eng.tensor_reduce(dst, src, AX.X, ALU.add)

            eng.wait_ge(s["x_in"], 32)
            both = [(xs, 0), (xs, 1), (ms, 0), (ms, 1)]
            for i, (src, t) in enumerate(both):
                do(eng.tensor_tensor_reduce(sqx, src[:, t, :], src[:, t, :], 1.0, 0.0, ALU.mult, ALU.add,
                                            stat[:, i:i + 1]))
                settle()
            do(ts(stat[:, 0:4], stat[:, 0:4], 1.0 / D, EPS, ALU.mult, ALU.add), s["xsq_done"])
            eng.wait_ge(s["const_in"], 32)
            do(ts(hw0, V("w0"), 0.5, None, ALU.mult))
            do(ts(ha0, V("a0"), 0.5, None, ALU.mult))
            do(ts(hbm, V("b_merge"), 0.5, None, ALU.mult))
            do(ts(omka, V("k_a"), -1.0, 1.0, ALU.mult, ALU.add))
            eng.wait_ge(s["xr_done"], 1)
            for i, (src, t) in enumerate(both):
                do(ts(src[:, t, :], src[:, t, :], rstd[:, i:i + 1], None, ALU.mult), s["xn_done"])
            for job, dst, gain in (("hT", hT, "g_mix"), ("mT", mT, "g_mem")):
                for t in range(TT):
                    for q in range(2):
                        full((job, q, t))
                        free(tt(dst[:, 4 * q:4 * q + 4, t * P:(t + 1) * P],
                                B((job, q, t)).rearrange("p (k n) -> p k n", k=4),
                                bc(V(gain)[:, 4 * q:4 * q + 4], 2, P), ALU.mult), (job, q, t))

            eng.wait_ge(s["R_zero"], 1)
            for ct in range(0, 14, 2):
                taken(eng, ("shift", ct))
                do(tt(pp[:, ct:ct + 2, :], pbuf[:, ct:ct + 2, 0:S], pbuf[:, ct:ct + 2, 1:S + 1], ALU.subtract))
                settle()
                for c in (ct, ct + 1):
                    do(stt(pp[:, c, :], pp[:, c, :], V("mix", c), pbuf[:, c, 1:S + 1], ALU.mult, ALU.add),
                       s["pp_done"])

            eng.wait_ge(s["small_in"], 144)
            eng.wait_ge(s["qk_sq"], 1)
            do(row_sum(rs, rot1.rearrange("p t h d -> p (t h) d")))
            settle()
            do(ts(rs, rs, 1.0 / DH, EPS, ALU.mult, ALU.add), s["qk_ss"])
            taken(eng, ("km", 1))
            for i, (src, t, h) in enumerate((src, t, h) for src in (qm, km) for t in range(TT) for h in range(MH)):
                do(eng.tensor_tensor_reduce(rot2[:, 0, 0:2, :].rearrange("p a b -> p (a b)"), src[:, t, h, :],
                                            src[:, t, h, :], 1.0, 0.0, ALU.mult, ALU.add, rsm[:, i:i + 1]))
                settle()
            do(ts(rsm, rsm, 1.0 / MD, EPS, ALU.mult, ALU.add), s["qm_sq"])
            eng.wait_ge(s["qk_r"], 1)
            flat = qk.rearrange("p t h d -> p (t h) d")
            do(tt(flat, flat, bc(rr, 2, DH), ALU.mult))
            settle()
            for t in range(TT):
                do(tt(qk[:, t], qk[:, t], nwt, ALU.mult))
            settle()
            half = DH // 2

            def rope(dst, src, a, b, cos, sin, heads):
                do(tt(a, src, bc(cos, 1, heads), ALU.mult))
                do(tt(b[..., 0:half], src[..., half:DH], bc(sin[:, 0:half], 1, heads), ALU.mult))
                do(tt(b[..., half:DH], src[..., 0:half], bc(sin[:, half:DH], 1, heads), ALU.mult))
                settle()

            for t in range(TT):
                rope(qk[:, t], qk[:, t], rot1[:, t], rot2[:, t], C("cos", 2)[:, t], C("sin", 2)[:, t], 12)
                do(tt(qk[:, t], rot1[:, t], rot2[:, t], ALU.add), s["qk_rot"])
            eng.wait_ge(s["qm_r"], 1)
            for i, src in enumerate((qm, km)):
                f = src.rearrange("p t h d -> p (t h) d")
                do(tt(f, f, bc(rrm[:, 8 * i:8 * i + 8], 2, MD), ALU.mult), s["qm_n"])

            do(cp(R[:, :, :, 30], pe_sb))
            full(("kcT",))
            src = B(("kcT",)).rearrange("p (j c l two) -> p j two l c", j=2, c=16, two=2)
            n = 0
            for g in range(NG):
                for par in range(2):
                    for h in range(2):
                        for j in range(2):
                            n += 1
                            ins_ = cp(R[DH * par:DH * par + DH, j, 8 * h:8 * h + 8, g * NC:(g + 1) * NC],
                                      src[DH * g:DH * g + DH, j, par, :, h:h + NC])
                            if n == 16:
                                free(ins_, ("kcT",))
                            else:
                                do(ins_)
            full(("hid",))
            hid = B(("hid",))[:, 0:64].rearrange("p (j c) -> p j c", j=2)
            do(tt(hbias, hid[:, :, 30], V("cmp_b1"), ALU.add))
            settle()
            free(tt(hx, hid[:, :, 0:30], bc(hbias, 2, 30), ALU.add), ("hid",))
            settle()
            do(tt(hu, hx, hx, ALU.mult))
            settle()
            do(ts(hu, hu, 0.044715, 1.0, ALU.mult, ALU.add))
            settle()
            do(tt(hu, hu, hx, ALU.mult), s["tanh_in"])
            eng.wait_ge(s["tanh_out"], 1)
            do(stt(ge, hu, 1.0, hx, ALU.add, ALU.mult))
            settle()
            do(ts(ge, ge, 0.5, None, ALU.mult), s["ge_done"])
            full(("cmp2",))
            free(cp(ctok.rearrange("p j g d -> p (j g d)"), B(("cmp2",), NC)[:, 0:4 * DH]), ("cmp2",))
            settle()
            do(tt(csq, ctok[:, 0], ctok[:, 0], ALU.mult))
            settle()
            do(row_sum(cs2, csq))
            settle()
            do(ts(cs2, cs2, 1.0 / DH, EPS, ALU.mult, ALU.add), s["kc_sq"])
            eng.wait_ge(s["kc_r"], 1)
            do(tt(ctok[:, 0], ctok[:, 0], bc(cr2, 2, DH), ALU.mult))
            settle()
            do(tt(ctok[:, 0], ctok[:, 0], bc(kn0, 1, NG), ALU.mult))
            settle()
            rope(None, ctok[:, 0], crot, csq, C("ccos", parts=NC), C("csin", parts=NC), NG)
            do(tt(ctok[:, 0], crot, csq, ALU.add), s["kc_rot"])

            for w, dst, gain in (("q", qmT, "mq_n"), ("k", kmT, "mk_n")):
                for t in range(TT):
                    full(("memT", w, t))
                    free(ts(dst[:, :, t * P:(t + 1) * P], B(("memT", w, t)).rearrange("p (h n) -> p h n", h=MH),
                            V(gain, 0), None, ALU.mult), ("memT", w, t))
            eng.wait_ge(s["gate_raw"], 1)
            do(ts(gates, gates, 0.5, 0.5, ALU.mult, ALU.add))

            def front(u):
                kind, h0, t, nh, nt = UNITS[u]
                nk = nt * P or NC
                b = B(("scores", u))[:, 0:nh * nk].rearrange("p (h k) -> p h k", h=nh)
                sc = sb_s[:, u % 2, 0:nh * nk].rearrange("p (h k) -> p h k", h=nh)
                full(("scores", u))
                if kind == "mem":
                    free(cp(sc, b), ("scores", u))
                else:
                    mask = C("cmpneg", 2)[:, t] if kind == "cmp" else C("causal")[:, (2 - nt) * P:2 * P]
                    free(tt(sc, b, bc(mask, 1, nh), ALU.add), ("scores", u))
                settle()
                do(row_max(mx[:, u % 2, 0:nh], sc))
                settle()
                scale = (MD if kind == "mem" else DH) ** -0.5
                do(ts(nmx[:, u % 2, 0:nh], mx[:, u % 2, 0:nh], -scale, None, ALU.mult), s["m_ready"])

            def factor(u):
                kind, h0, t, nh, nt = UNITS[u]
                total, f = sm[:, u % 2, 0:nh], fac[:, u % 2, 0:nh]
                eng.wait_ge(s["e_ready"], u + 1)
                if kind == "cmp":
                    e = sb_e[:, u % 2, 0:nh * NC].rearrange("p (h k) -> p h k", h=nh)
                    do(tt(e, e, bc(C("cmpok", 2)[:, t], 1, nh), ALU.mult), s["cmp_ok"])
                    settle()
                    do(row_sum(total, e))
                    settle()
                    do(ts(total, total, 1e-30, None, ALU.max))
                    settle()
                do(eng.reciprocal(f, total))
                settle()
                if kind != "mem":
                    h = 4 * h0 if kind == "cmp" else h0
                    g3 = gates[:, t, :].rearrange("p (h b) -> p h b", b=3)
                    do(tt(f, f, g3[:, h:h + nh, ("cmp", "slc", "win").index(kind)], ALU.mult))
                    settle()

            def gather(u):
                kind, h0, t, nh, nt = UNITS[u]
                dv = MD if kind == "mem" else DH
                h = 4 * h0 if kind == "cmp" else h0
                full(("values", u))
                b = B(("values", u))[:, 0:nh * dv].rearrange("p (h d) -> p h d", h=nh)
                f = bc(fac[:, u % 2, 0:nh], 2, dv)
                if kind == "mem":
                    free(tt(omem[:, t, h:h + nh, :], b, f, ALU.mult), ("values", u))
                elif kind == "cmp":
                    free(tt(osum[:, t, h:h + nh, :], b, f, ALU.mult), ("values", u))
                else:
                    part = otmp[:, u % 2, 0:nh * dv].rearrange("p (h d) -> p h d", h=nh)
                    free(tt(part, b, f, ALU.mult), ("values", u))
                    settle()
                    do(tt(osum[:, t, h:h + nh, :], osum[:, t, h:h + nh, :], part, ALU.add))

            front(0)
            front(1)
            for u in range(len(UNITS)):
                factor(u)
                if u + 2 < len(UNITS):
                    front(u + 2)
                gather(u)
            settle()
            do(ts(stat[:, 6:7], stat[:, 0:1], 1.0, None, ALU.mult), s["values_done"])

            r_, k_, v_ = pp[:, 0:4, :], pp[:, 4:8, :], pp[:, 8:12, :]
            taken(eng, ("omT", 1))
            eng.wait_ge(s["wa_done"], 2)
            do(ts(pp[:, 13, :], pp[:, 13, :], 0.5, 0.5, ALU.mult, ALU.add), s["xg_done"])
            do(eng.memset(dE[:, :, 0:1], 0.0))
            do(eng.memset(pat, 0.0))
            settle()
            pat3 = pat.rearrange("p (a b) -> p a b", a=16)
            do(eng.memset(pat3[:, :, 0:1], 1.0))
            do(tt(kkn, k_, bc(V("k_k"), 2, S), ALU.mult))
            eng.wait_ge(s["decay_done"], 1)
            settle()
            do(eng.tensor_tensor_scan(Dc.rearrange("p a b -> p (a b)"), dE.rearrange("p a b -> p (a b)"), pat, 0.0,
                                      ALU.mult, ALU.add))
            do(tt(tmp, kkn, kkn, ALU.mult), s["k_sq"])
            taken(eng, ("up", "a", 1))
            do(ts(aa, aa, 0.5, 0.5, ALU.mult, ALU.add))
            taken(eng, ("ksum", 1))
            do(ts(Di, Di, 1e-12, None, ALU.max))
            settle()
            do(eng.reciprocal(Di, Di))
            do(tt(tmp, aa, bc(V("k_a"), 2, S), ALU.mult))
            settle()
            do(tt(kkn, kkn, Di, ALU.mult))
            do(tt(tmp, tmp, bc(omka, 2, S), ALU.add))
            settle()
            do(tt(k_, k_, tmp, ALU.mult))
            do(tt(aa, aa, kkn, ALU.mult))
            dnow = Dc[:, :, 1:CH + 1]
            dprev = Dc[:, :, 0:CH]

            def chunks(ap):
                return ap.rearrange("p j (c n) -> p (j c) n", n=CH)

            do(eng.reciprocal(chunks(Di), dnow))
            settle()
            do(tt(tmp, r_, k_, ALU.mult))
            settle()
            do(tt(tmp, tmp, bc(V("r_k"), 2, S), ALU.mult), s["rk_done"])
            for hh in range(2):
                lanes = slice(DH * hh, DH * hh + DH)

                def ch(ap):
                    return ap.rearrange("p (j c) n -> p j c n", j=4)[lanes]

                for j in range(4):
                    o = {w: til[w][:, 2 * j + hh, :].rearrange("p (c n) -> p c n", n=CH) for w in "abkr"}

                    def at(ap):
                        return ap[lanes, j, :].rearrange("p (c n) -> p c n", n=CH)

                    do(stt(o["a"], at(kkn), -1.0, ch(dprev)[:, j], ALU.mult, ALU.mult), s["tilde_done"])
                    do(tt(o["b"], at(aa), at(Di), ALU.mult), s["tilde_done"])
                    do(tt(o["k"], at(k_), at(Di), ALU.mult), s["tilde_done"])
                    do(tt(o["r"], at(r_), ch(dnow)[:, j], ALU.mult), s["tilde_done"])
                do(cp(DC.rearrange("p (j two) c -> p two j c", two=2)[:, hh],
                      ch(Dc)[:, :, :, CH:CH + 1].rearrange("p j c n -> p j (c n)")))
            for q in range(2):
                full(("bonus", q))
                free(tt(bon[:, 2 * q:2 * q + 2, :], B(("bonus", q)).rearrange("p (j s) -> p j s", j=2),
                        v_[:, 2 * q:2 * q + 2, :], ALU.mult), ("bonus", q))

            settle()
            for X in (Mm, Tm):
                do(cp(X, bc(ident, 1, 16)))
            settle()

            def four(ap, b):
                return ap[:, 4 * b:4 * b + 4, :]

            def bank4(job):
                return B(job).rearrange("p (h n) -> p h n", h=4)

            for b in range(4):
                full(("A", b))
                do(tt(four(Am, b), bank4(("A", b)), bc(C("low"), 1, 4), ALU.mult))
                free(eng.copy_predicated(four(Tm, b), bc(C("lo1"), 1, 4).bitcast(U32), bank4(("A", b))), ("A", b))
            for b in range(4):
                full(("B", b))
                free(eng.copy_predicated(four(Mm, b), bc(C("up1"), 1, 4).bitcast(U32), bank4(("B", b))), ("B", b))
            for w, dst, mask in (("Kk", Kk, "upp"), ("Rb", Rb, "uppi"), ("Rk", Rk, "uppi")):
                for b in range(4):
                    full((w, b))
                    free(tt(four(dst, b), bank4((w, b)), bc(C(mask), 1, 4), ALU.mult), (w, b))
            for n in LEVELS:
                for b in range(4):
                    full(("MX", n, b))
                    free(eng.copy_predicated(four(Mm, b), bc(C(f"up{n}"), 1, 4).bitcast(U32), bank4(("MX", n, b))),
                         ("MX", n, b))
                    if n < 32:
                        full(("XT", n, b))
                        free(eng.copy_predicated(four(Tm, b), bc(C(f"lo{n}"), 1, 4).bitcast(U32),
                                                 bank4(("XT", n, b))), ("XT", n, b))
            for b in range(4):
                t, hq = divmod(b, 2)
                full(("rhat", b))
                r3 = til["r"][:, 4 * hq:4 * hq + 4, t * P:(t + 1) * P]
                free(tt(r3, r3, B(("rhat", b), DH).rearrange("p (h n) -> p h n", h=4), ALU.add), ("rhat", b))
            taken(eng, ("Q", 0))
            do(tt(Ss[:, 0], Qs[:, 0], bc(DC[:, :, 0], 2, DH), ALU.mult), s["state_done"])
            for c in (1, 2):
                taken(eng, ("Q", c))
                full(("state", c))
                free(tt(stmp, B(("state", c), DH).rearrange("p (h n) -> p h n", h=NH), Qs[:, c], ALU.add),
                     ("state", c))
                settle()
                do(tt(stmp, stmp, Ss[:, c - 1], ALU.add))
                settle()
                do(tt(Ss[:, c], stmp, bc(DC[:, :, c], 2, DH), ALU.mult), s["state_done"])
            for q in range(2):
                full(("mean", q))
                yv = yb[:, 2 * q:2 * q + 2, :]
                free(stt(yv, B(("mean", q)).rearrange("p (j s) -> p j s", j=2), -1.0 / DH, yv, ALU.mult, ALU.add),
                     ("mean", q))
            settle()
            do(tt(yq, yb, yb, ALU.mult), s["y_sq"])
            taken(eng, ("var", 1))
            do(eng.reciprocal(yq, yq))
            settle()
            do(tt(yb, yb, yq, ALU.mult))
            settle()
            do(tt(yb, yb, bc(V("ln_w"), 2, S), ALU.mult))
            settle()
            do(tt(yb, yb, bc(V("ln_b"), 2, S), ALU.add))
            settle()
            do(tt(yb, yb, bon, ALU.add))
            settle()
            do(tt(obT, yb, gg, ALU.mult), s["ob_done"])

            for n in range(3):
                for ct in range(0, KD, 2):
                    job = ("branch", n, ct)
                    full(job)
                    taken(eng, ("merge", n * KD + ct))
                    b = B(job).rearrange("p (j s) -> p j s", j=2)
                    g2 = tg[:, n * KD + ct:n * KD + ct + 2, :]
                    if n == 0:
                        free(stt(mixT[:, ct:ct + 2, :], g2, 1.0, b, ALU.add, ALU.mult), job)
                    else:
                        prod = mprod[:, ct // 2 % 2, :].rearrange("p (j s) -> p j s", j=2)
                        free(stt(prod, g2, 1.0, b, ALU.add, ALU.mult), job)
                        settle()
                        do(tt(mixT[:, ct:ct + 2, :], mixT[:, ct:ct + 2, :], prod, ALU.add), s["mix_done"])
            eng.wait_ge(s["late_in"], 32)
            for t in range(TT):
                for q in range(2):
                    full(("out", t, q))
                    xv = x1[:, t, q * 512:(q + 1) * 512]
                    free(stt(xv, B(("out", t, q)), 0.5, xv, ALU.mult, ALU.add), ("out", t, q))
                    settle()
            for t in range(TT):
                do(eng.tensor_tensor_reduce(tg[:, 0:4, :].rearrange("p a b -> p (a b)"), x1[:, t, :], x1[:, t, :],
                                            1.0, 0.0, ALU.mult, ALU.add, stat[:, 4 + t:5 + t]))
                settle()
            do(ts(stat[:, 4:6], stat[:, 4:6], 1.0 / D, EPS, ALU.mult, ALU.add), s["x1_sq"])
            eng.wait_ge(s["x1_r"], 1)
            for t in range(TT):
                do(ts(xn2[:, t, :], x1[:, t, :], rstd[:, 4 + t:5 + t], None, ALU.mult), s["xn2_done"])
            for t in range(TT):
                for q in range(2):
                    job = ("h2T", q, t)
                    full(job)
                    free(tt(h2T[:, 4 * q:4 * q + 4, t * P:(t + 1) * P], B(job).rearrange("p (k n) -> p k n", k=4),
                            bc(V("g_ffn")[:, 4 * q:4 * q + 4], 2, P), ALU.mult), job)

            full(("logits",))
            free(cp(lg.rearrange("p t e -> p (t e)"), B(("logits",))[:, 0:TT * NE]), ("logits",))
            settle()
            for t in range(TT):
                do(eng.max(top[:, t, :], lg[:, t, :]))
                settle()
                do(eng.max_index(idx[:, t, :], top[:, t, :], lg[:, t, :]))
            settle()
            do(cp(idf, idx))
            do(tt(et, top[:, :, 0:TOPK], bc(top[:, :, 0], 2, TOPK), ALU.subtract), s["lg_ss"])
            eng.wait_ge(s["lg_exp"], 1)
            do(row_sum(es, et))
            settle()
            do(eng.reciprocal(er, es))
            settle()
            do(tt(et, et, bc(er, 2, TOPK), ALU.mult))
            settle()
            for t in range(TT):
                for k in range(TOPK):
                    one = idf[:, t, k:k + 1]
                    dst = gat[:, t, :] if k == 0 else rk1[:, t, :]
                    do(ts(dst, C("experts"), one, et[:, t, k:k + 1], ALU.is_equal, ALU.mult))
                    if k == 0:
                        do(ts(sel[:, t, :], C("experts"), one, None, ALU.is_equal))
                    else:
                        do(stt(sel[:, t, :], C("experts"), one, sel[:, t, :], ALU.is_equal, ALU.add))
                        settle()
                        do(tt(gat[:, t, :], gat[:, t, :], rk1[:, t, :], ALU.add))
                    settle()
            do(cp(nz, C("half")[:, 0:2]), s["sel_done"])
            full(("rank",))
            rank = B(("rank",))[:, 0:TT * NE].rearrange("p (t e) -> p t e", t=TT)
            do(stt(rk1, rank, 1.0, sel, ALU.add, ALU.mult))
            free(row_max(cm[:, 0:1], B(("rank",))[:, TT * NE:(TT + 1) * NE]), ("rank",))
            settle()
            for r in range(ROUNDS):
                do(ts(rankR[:, :, r * NE:(r + 1) * NE], rk1, -1.0 - CAP * r, None, ALU.add))
                do(ts(gateR[:, :, r * NE:(r + 1) * NE], gat, 0.5, None, ALU.mult))
            do(eng.memset(rankR[:, :, ROUNDS * NE:], -1.0))
            do(eng.memset(gateR[:, :, ROUNDS * NE:], 0.0))
            for r in range(1, ROUNDS):
                do(ts(cm[:, r:r + 1], cm[:, 0:1], float(CAP * r), None, ALU.is_gt))
            settle()
            do(row_sum(cm[:, 4:5], cm[:, 1:ROUNDS]))
            settle()
            do(ts(nrounds, cm[:, 4:5], 1.0, None, ALU.add))
            do(eng.memset(osb, 0.0))
            do(eng.memset(pgt, 0.0))
            settle()
            taken(eng, ("gateT",))
            eng.sem_inc(s["o_free"], 1)
            eng.sem_inc(s["t_out"], 1)
            eng.sem_inc(s["h_out"], 2)
            for k in range(2):
                for t in range(TT):
                    ins_ = ts(Pk[:, t, k, :], C("slots"), rankR[:, t, k:k + 1], None, ALU.is_equal)
                    do(ins_, s["P_ready"]) if (k, t) == (1, TT - 1) else do(ins_)
            do(cp(nz, C("half")[:, 0:2]), s["scratch_free"])
            settle()

            def take(number):
                eng.wait_ge(s["g_full"], number)
                eng.tensor_tensor(xg.rearrange("p (b k) n -> p b k n", b=2),
                                  psum[:, 4:6, :].rearrange("p b (k n) -> p b k n", k=4),
                                  bc(V("g_ffn").rearrange("p (b k) -> p b k", b=2), 3, 2 * CAP),
                                  ALU.mult).then_inc(s["xg_ready"], 1)

            take(1)
            rounds = load_rounds(eng)
            with eng.Fori(0, rounds) as r:
                with eng.Fori(0, NE // 2) as i:
                    it = r * (NE // 2) + i
                    for k in range(2):
                        E = it * 2 + k
                        for t in range(TT):
                            for twice in range(2):
                                x_ = eng.tensor_scalar(PG[:, t, twice, :], C("slots"), rankR[:, t, bass.ds(E, 1)],
                                                       gateR[:, t, bass.ds(E, 1)], ALU.is_equal, ALU.mult)
                        x_.then_inc(s["pg_ready"], 1)
                        if k == 0:
                            for n in range(2):
                                for t in range(TT):
                                    x_ = eng.tensor_scalar(Pk[:, t, n, :], C("slots"),
                                                           rankR[:, t, bass.ds(it * 2 + (2 + n), 1)], None,
                                                           ALU.is_equal)
                            x_.then_inc(s["P_ready"], 1)
                        eng.wait_ge(s["t_full"], E * 5 + 1)
                        eng.tensor_copy(pgt[:, k, :], psum[:, 5, 0:S]).then_inc(s["t_out"], 1)
                        for q in range(4):
                            hf = q % 2
                            eng.wait_ge(s["t_full"], E * 5 + (q + 2))
                            bias = b1_sb[:, bass.ds(i * 2 + k, 1), 4 * q:4 * q + 4].rearrange("p e n -> p (e n)")
                            eng.tensor_tensor(hb[:, hf, :].rearrange("p (a n) -> p a n", a=4),
                                              psum[:, 5, 0:4 * CAP].rearrange("p (a n) -> p a n", a=4),
                                              bc(bias, 2, CAP), ALU.add).then_inc(s["t_out"], 1)
                            eng.wait_ge(s["t_out"], E * 5 + (q + 3))
                            eng.tensor_scalar(xlo[:, hf, :], hb[:, hf, 0:2 * CAP], 7.0, None, ALU.min
                                              ).then_inc(s["x_ready"], 1)
                            eng.tensor_scalar(xhi[:, hf, :], hb[:, hf, 2 * CAP:4 * CAP], 7.0, -7.0, ALU.min, ALU.max
                                              ).then_inc(s["v2_step"], 1)
                            eng.wait_ge(s["t_ready"], E * 4 + (q + 1))
                            eng.scalar_tensor_tensor(out=th[:, hf, :], in0=th[:, hf, :], scalar=1.0,
                                                     in1=xlo[:, hf, :], op0=ALU.add, op1=ALU.mult
                                                     ).then_inc(s["v2_step"], 1)
                            eng.wait_ge(s["v2_step"], E * 8 + (2 * q + 2))
                            eng.scalar_tensor_tensor(
                                out=act[:, 2 * q:2 * q + 2, :].rearrange("p a n -> p (a n)"), in0=xhi[:, hf, :],
                                scalar=1.0, in1=th[:, hf, :], op0=ALU.add, op1=ALU.mult).then_inc(s["a_ready"], 1)
                        if k == 1:
                            take(it + 2)
            eng.wait_ge(s["y_full"], 1)
            for t in range(TT):
                eng.tensor_tensor(x1[:, t, :].rearrange("p (a n) -> p a n", a=2), psum[:, 2 * t:2 * t + 2, :],
                                  x1[:, t, :].rearrange("p (a n) -> p a n", a=2), ALU.add).then_inc(s["y_out"], 1)

        @block.scalar
        def _(eng):
            a = Steps(eng, s["a_step"], bank_free, bank_full)
            do, free, full, settle = a.do, a.free, a.full, a.settle
            act_, cp = eng.activation, eng.copy

            def halves(job, n=2):
                return B(job).rearrange("p (j s) -> p j s", j=n)

            for ct in range(0, 14, 2):
                full(("shift", ct))
                free(cp(pbuf[:, ct:ct + 2, 1:S + 1], halves(("shift", ct))), ("shift", ct))
            for t in range(TT):
                full(("q", t))
                free(cp(qk[:, t, 0:NH, :].rearrange("p h d -> p (h d)"), B(("q", t))), ("q", t))
            for t in range(TT):
                full(("kc", t))
                do(cp(qk[:, t, NH:12, :].rearrange("p h d -> p (h d)"), B(("kc", t))[:, 0:256]))
                free(cp(kcv[:, t].rearrange("p j n -> p (j n)"), B(("kc", t))[:, 256:512]), ("kc", t))
            for t in range(TT):
                full(("vg", t))
                free(cp(vg[:, t, :], B(("vg", t))[:, 0:280]), ("vg", t))
            for w, dst in (("qm", qm), ("km", km), ("vm", vm)):
                for t in range(TT):
                    full((w, t))
                    free(cp(dst[:, t].rearrange("p h d -> p (h d)"), B((w, t))), (w, t))
            settle()
            do(act_(gates, vg[:, :, 256:280], ACT.Tanh, scale=0.5), s["gate_raw"])
            eng.wait_ge(s["tanh_in"], 1)
            do(act_(hu, hu, ACT.Tanh, scale=0.7978845608028654), s["tanh_out"])
            full(("cT",))
            free(cp(kcT, B(("cT",), DH)[:, 0:2 * NC].rearrange("p (g c) -> p g c", g=2)), ("cT",))
            for t in range(TT):
                for q in range(3):
                    full(("qkT", t, q))
                    free(cp(qkT[:, 4 * q:4 * q + 4, t * P:(t + 1) * P],
                            B(("qkT", t, q), DH).rearrange("p (h n) -> p h n", h=4)), ("qkT", t, q))

            def exps(u):
                kind, h0, t, nh, nt = UNITS[u]
                nk = nt * P or NC
                scale = (MD if kind == "mem" else DH) ** -0.5
                eng.wait_ge(s["m_ready"], u + 1)
                for h in range(nh):
                    ins_ = act_(sb_e[:, u % 2, h * nk:(h + 1) * nk], sb_s[:, u % 2, h * nk:(h + 1) * nk], ACT.Exp,
                                bias=nmx[:, u % 2, h:h + 1], scale=scale, accum_out=sm[:, u % 2, h:h + 1])
                    do(ins_, s["e_ready"]) if h == nh - 1 else do(ins_)

            exps(0)
            exps(1)
            for u in range(len(UNITS)):
                full(("turn", u))
                if u >= 2:
                    full(("values", u - 2))
                rows = P if UNITS[u][4] else NC
                free(cp(sb_eT[0:rows, u % 2, :], B(("turn", u), rows)), ("turn", u))
                if u + 2 < len(UNITS):
                    exps(u + 2)
            for w, dst in (("oaT", oaT), ("omT", omT)):
                for t in range(TT):
                    full((w, t))
                    free(cp(dst[:, :, t * P:(t + 1) * P], B((w, t)).rearrange("p (c n) -> p c n", c=4)), (w, t))

            eng.wait_ge(s["pp_done"], 14)
            do(act_(pp[0:DH, 12, :], pp[0:DH, 12, :], ACT.Tanh), s["wa_done"])
            do(act_(pp[:, 13, :], pp[:, 13, :], ACT.Tanh, scale=0.5), s["wa_done"])
            for q in range(2):
                full(("up", "w", q))
                for c in range(2):
                    ins_ = act_(tmp[:, 2 * q + c, :], halves(("up", "w", q))[:, c, :], ACT.Tanh,
                                bias=hw0[:, 2 * q + c:2 * q + c + 1], scale=0.5)
                    free(ins_, ("up", "w", q)) if c else do(ins_)
            settle()
            do(act_(tmp, tmp, ACT.Copy, scale=-EM05 / 2, bias=-EM05 / 2))
            settle()
            do(act_(dE[:, :, 1:CH + 1], tmp.rearrange("p j (c n) -> p (j c) n", n=CH), ACT.Exp), s["decay_done"])
            for q in range(2):
                full(("up", "a", q))
                for c in range(2):
                    ins_ = act_(aa[:, 2 * q + c, :], halves(("up", "a", q))[:, c, :], ACT.Tanh,
                                bias=ha0[:, 2 * q + c:2 * q + c + 1], scale=0.5)
                    free(ins_, ("up", "a", q)) if c else do(ins_)
            for q in range(2):
                full(("up", "g", q))
                free(cp(gg[:, 2 * q:2 * q + 2, :], halves(("up", "g", q))), ("up", "g", q))
            for q in range(2):
                full(("ksum", q))
                free(act_(Di[:, 2 * q:2 * q + 2, :], halves(("ksum", q)), ACT.Sqrt), ("ksum", q))
            for t in range(TT):
                full(("vtok", t))
                free(cp(tok["v"][:, t].rearrange("p h d -> p (h d)"), B(("vtok", t))), ("vtok", t))
            for w in "akb":
                for t in range(TT):
                    full(("tok", w, t))
                    b = B(("tok", w, t)).rearrange("p (h d) -> p h d", h=NH)
                    dst = KA[:, t * NH:(t + 1) * NH, DH:P] if w == "a" else tok[w][:, t]
                    free(cp(dst, b), ("tok", w, t))
            for t in range(TT):
                full(("KV", t))
                free(cp(KA[:, t * NH:(t + 1) * NH, 0:DH], B(("KV", t)).rearrange("p (h d) -> p h d", h=NH)), ("KV", t))
            for n in LEVELS:
                for b in range(4):
                    full(("X", n, b))
                    free(cp(Xm[:, b, :], B(("X", n, b))), ("X", n, b))
            for b in range(4):
                full(("UW", b))
                free(cp(UW[:, 4 * b:4 * b + 4, :], B(("UW", b)).rearrange("p (h n) -> p h n", h=4)), ("UW", b))
            for w, c in (("Q", 0), ("Q", 1), ("PT", 1), ("Q", 2), ("PT", 2)):
                full((w, c))
                dst = Qs if w == "Q" else PT
                free(cp(dst[:, c], B((w, c), DH).rearrange("p (h n) -> p h n", h=NH)), (w, c))
            for t in range(TT):
                full(("Y", t))
                free(cp(yb[:, :, t * P:(t + 1) * P], B(("Y", t)).rearrange("p (j n) -> p j n", j=4)), ("Y", t))
            for q in range(2):
                full(("var", q))
                free(act_(yq[:, 2 * q:2 * q + 2, :], halves(("var", q)), ACT.Sqrt, scale=1.0 / DH,
                          bias=C("gn_eps")), ("var", q))

            eng.wait_ge(s["ob_done"], 1)
            for ct in range(0, MERGE_T, 2):
                full(("merge", ct))
                for c in range(2):
                    ins_ = act_(tg[:, ct + c, :], halves(("merge", ct))[:, c, :], ACT.Tanh,
                                bias=hbm[:, ct + c:ct + c + 1], scale=0.5)
                    free(ins_, ("merge", ct)) if c else do(ins_)
            eng.wait_ge(s["lg_ss"], 1)
            do(act_(et, et, ACT.Exp), s["lg_exp"])
            full(("gateT",))
            free(cp(gT[0:NE, :], B(("gateT",), NE)[:, 0:S]), ("gateT",))

            rounds = load_rounds(eng)
            with eng.Fori(0, rounds) as r:
                with eng.Fori(0, NE // 2) as i:
                    for k in range(2):
                        E = (r * (NE // 2) + i) * 2 + k

                        def evacuate(q):
                            eng.wait_ge(s["h_full"], E * 4 + (q + 5))
                            cp(hraw[:, q % 2, :], psum[:, 6 + q % 2, :]).then_inc(s["h_out"], 1)

                        evacuate(0)
                        for q in range(4):
                            if q < 3:
                                evacuate(q + 1)
                            eng.wait_ge(s["x_ready"], E * 4 + (q + 1))
                            act_(th[:, q % 2, :], xlo[:, q % 2, :], ACT.Tanh, scale=1.702 / 2
                                 ).then_inc(s["t_ready"], 1)
                        eng.wait_ge(s["o_full"], E + 2)
                        cp(osb, psum[:, 4:6, :].rearrange("p a n -> p (a n)")).then_inc(s["o_free"], 1)

        @block.tensor
        def _(pe):
            def use(job):
                b, used = BANK[job]
                if used:
                    pe.wait_ge(bank_free[b], used)

            def fill(ins_, job):
                ins_.then_inc(bank_full[BANK[job][0]], 1)

            def weights(name):
                n = W1_AT[name]
                pe.wait_ge(w1_in[n % N1], 16 * (n // N1 + 1))
                return slots[n % N1]

            def mm(o, lhsT, rhs, start=True, stop=True):
                return pe.matmul(o, lhsT, rhs, start=start, stop=stop, skip_group_check=True)

            def turn(o, in_):
                return pe.transpose(o, in_, ident[0:in_.shape[0], 0:in_.shape[0]])

            pe.wait_ge(s["const_in"], 32)
            for j, (w, src) in enumerate((("hT", xs), ("mT", ms))):
                for t in range(TT):
                    pe.wait_ge(s["xn_done"], 2 * j + t + 1)
                    for q in range(2):
                        job = (w, q, t)
                        use(job)
                        for k in range(4):
                            last = turn(B(job)[:, k * P:(k + 1) * P],
                                        src[:, t, (4 * q + k) * P:(4 * q + k + 1) * P])
                        fill(last, job)
            for t in range(TT):
                for q in range(2):
                    taken(pe, ("hT", q, t))

            def channel_major(jobs, unit):
                w = weights(unit).rearrange("p (k n) -> p k n", k=KD)
                for c0, job in jobs:
                    use(job)
                    for c in range(2):
                        for k in range(KD):
                            last = mm(B(job)[:, c * S:(c + 1) * S], w[:, k, (c0 + c) * P:(c0 + c + 1) * P],
                                      hT[:, k, :], k == 0, k == KD - 1)
                    fill(last, job)

            for n, (c0, nc_) in enumerate(SHIFT_UNITS):
                channel_major([(c, ("shift", c0 + c)) for c in range(0, nc_, 2)], f"shift{n}")
            for name in ("q", "kc", "vg", "qm", "km", "vm"):
                w = weights(name).rearrange("p (k n) -> p k n", k=KD)
                src = mT if name in ("km", "vm") else hT
                if name == "km":
                    for t in range(TT):
                        for q in range(2):
                            taken(pe, ("mT", q, t))
                width = 280 if name == "vg" else 512
                for t in range(TT):
                    use((name, t))
                    for k in range(KD):
                        last = mm(B((name, t))[:, 0:width], src[:, k, t * P:(t + 1) * P], w[:, k, 0:width],
                                  k == 0, k == KD - 1)
                    fill(last, (name, t))

            use(("kcT",))
            taken(pe, ("kc", 1))
            for j in range(2):
                for t in range(TT):
                    last = turn(B(("kcT",))[:, j * S + t * P:j * S + (t + 1) * P], kcv[:, t, j, :])
            fill(last, ("kcT",))
            use(("hid",))
            taken(pe, ("kcT",))
            pe.wait_ge(s["small_in"], 144)
            w = weights("cmp1").rearrange("p (j l n) -> p j l n", j=2, l=16)
            for j in range(2):
                for l in range(16):
                    last = mm(B(("hid",))[:, j * 32:j * 32 + 31], w[:, j, l, :], R[:, j, l, :], l == 0, l == 15)
            fill(last, ("hid",))
            use(("cmp2",))
            pe.wait_ge(s["ge_done"], 1)
            for j in range(2):
                for g in range(NG):
                    last = mm(B(("cmp2",), NC)[:, (2 * j + g) * DH:(2 * j + g + 1) * DH],
                              ge[:, j, g * NC:(g + 1) * NC], cw2[:, j, :])
            fill(last, ("cmp2",))
            use(("cT",))
            pe.wait_ge(s["kc_rot"], 1)
            for g in range(NG):
                last = turn(B(("cT",), DH)[:, g * NC:(g + 1) * NC], ctok[:, 0, g, :])
            fill(last, ("cT",))
            for t in range(TT):
                pe.wait_ge(s["qk_rot"], t + 1)
                for q in range(3):
                    use(("qkT", t, q))
                    for h in range(4):
                        last = turn(B(("qkT", t, q), DH)[:, h * P:(h + 1) * P], qk[:, t, 4 * q + h, :])
                    fill(last, ("qkT", t, q))
            pe.wait_ge(s["qm_n"], 2)
            for w, src in (("q", qm), ("k", km)):
                for t in range(TT):
                    use(("memT", w, t))
                    for h in range(MH):
                        last = turn(B(("memT", w, t))[:, h * P:(h + 1) * P], src[:, t, h, :])
                    fill(last, ("memT", w, t))

            taken(pe, ("cT",))
            for t in range(TT):
                for q in range(3):
                    taken(pe, ("qkT", t, q))
                taken(pe, ("memT", "q", t))
                taken(pe, ("memT", "k", t))

            def scores(u):
                kind, h0, t, nh, nt = UNITS[u]
                nk = nt * P or NC
                use(("scores", u))
                for h in range(nh):
                    if kind == "mem":
                        q_, k_ = qmT[:, h0 + h, t * P:(t + 1) * P], kmT[:, h0 + h, 0:nk]
                    elif kind == "cmp":
                        q_, k_ = qkT[:, 4 * h0 + h, t * P:(t + 1) * P], kcT[:, h0, :]
                    else:
                        kv = NH + (0 if kind == "slc" else NG) + h0 // 4
                        q_, k_ = qkT[:, h0 + h, t * P:(t + 1) * P], qkT[:, kv, 0:nk]
                    last = mm(B(("scores", u))[:, h * nk:(h + 1) * nk], q_, k_)
                fill(last, ("scores", u))

            scores(0)
            scores(1)
            for u, (kind, h0, t, nh, nt) in enumerate(UNITS):
                use(("turn", u))
                pe.wait_ge(s["e_ready"], u + 1)
                if kind == "cmp":
                    pe.wait_ge(s["cmp_ok"], u + 1)
                rows = P if nt else NC
                for b in range(4):
                    last = turn(B(("turn", u), rows)[:, b * P:(b + 1) * P], sb_e[:, u % 2, b * rows:(b + 1) * rows])
                fill(last, ("turn", u))
                if u + 2 < len(UNITS):
                    scores(u + 2)
                use(("values", u))
                taken(pe, ("turn", u))
                dv = MD if kind == "mem" else DH
                for h in range(nh):
                    for kt in range(nt or 1):
                        if kind == "mem":
                            val = vm[:, kt, h0 + h, :]
                        elif kind == "cmp":
                            val = ctok[:, 1, h0, :]
                        else:
                            c = (0 if kind == "slc" else P) + h0 // 4 * DH
                            val = vg[:, kt, c:c + DH]
                        blk = h * (nt or 1) + kt
                        last = mm(B(("values", u))[:, h * dv:(h + 1) * dv],
                                  sb_eT[0:rows, u % 2, blk * P:(blk + 1) * P], val, kt == 0, kt == (nt or 1) - 1)
                fill(last, ("values", u))
            pe.wait_ge(s["values_done"], 1)
            for w, src in (("oaT", osum), ("omT", omem)):
                for t in range(TT):
                    use((w, t))
                    flat = src[:, t].rearrange("p h d -> p (h d)")
                    for c in range(4):
                        last = turn(B((w, t))[:, c * P:(c + 1) * P], flat[:, c * P:(c + 1) * P])
                    fill(last, (w, t))

            for w in "wag":
                if w == "w":
                    pe.wait_ge(s["wa_done"], 1)
                if w == "g":
                    pe.wait_ge(s["xg_done"], 1)
                lanes = {"w": slice(0, DH), "a": slice(DH, P), "g": slice(0, P)}[w]
                for q in range(2):
                    use(("up", w, q))
                    for c in range(2):
                        ct = 2 * q + c
                        last = mm(B(("up", w, q))[:, c * S:(c + 1) * S],
                                  (up_g if w == "g" else up_w)[lanes, ct * P:(ct + 1) * P],
                                  pp[lanes, 13 if w == "g" else 12, :])
                    fill(last, ("up", w, q))
            flat = tmp.rearrange("p j s -> p (j s)")
            for w, ready in (("ksum", s["k_sq"]), ("bonus", s["rk_done"])):
                pe.wait_ge(ready, 1)
                for q in range(2):
                    use((w, q))
                    fill(mm(B((w, q)), C("heads"), flat[:, q * 512:(q + 1) * 512]), (w, q))
            for t in range(TT):
                use(("vtok", t))
                for j in range(4):
                    last = turn(B(("vtok", t))[:, j * P:(j + 1) * P], pp[:, 8 + j, t * P:(t + 1) * P])
                fill(last, ("vtok", t))
            pe.wait_ge(s["tilde_done"], 32)
            for w in "akb":
                for t in range(TT):
                    use(("tok", w, t))
                    for h in range(NH):
                        last = turn(B(("tok", w, t))[:, h * DH:(h + 1) * DH], til[w][:, h, t * P:(t + 1) * P])
                    fill(last, ("tok", w, t))
            for w, left, right in (("A", "a", "b"), ("B", "b", "a"), ("Kk", "k", "a"), ("Rb", "b", "r"),
                                   ("Rk", "k", "r")):
                for b in range(4):
                    t, hq = divmod(b, 2)
                    use((w, b))
                    for h in range(4):
                        tok_ = slice(t * P, (t + 1) * P)
                        last = mm(B((w, b))[:, h * P:(h + 1) * P], til[left][:, 4 * hq + h, tok_],
                                  til[right][:, 4 * hq + h, tok_])
                    fill(last, (w, b))
            for t in range(TT):
                use(("KV", t))
                for b in range(2):
                    taken(pe, ("Kk", 2 * t + b))
                taken(pe, ("vtok", t))
                for h in range(NH):
                    last = mm(B(("KV", t))[:, h * DH:(h + 1) * DH], Kk[:, t * NH + h, :], tok["v"][:, t, h, :])
                fill(last, ("KV", t))

            before = None
            for n in LEVELS:
                for b in range(4):
                    use(("X", n, b))
                    taken(pe, ("MX", before, b) if before else ("B", b))
                    for h in range(4):
                        last = mm(B(("X", n, b))[:, h * P:(h + 1) * P], Am[:, 4 * b + h, :], Mm[:, 4 * b + h, :])
                    fill(last, ("X", n, b))
                for b in range(4):
                    taken(pe, ("X", n, b))
                    if before:
                        taken(pe, ("XT", before, b))
                    for w in ("MX", "XT") if n < 32 else ("MX",):
                        use((w, n, b))
                        for h in range(4):
                            xh = Xm[:, b, h * P:(h + 1) * P]
                            th_ = Tm[:, 4 * b + h, :]
                            o = B((w, n, b))[:, h * P:(h + 1) * P]
                            last = mm(o, th_, xh) if w == "MX" else mm(o, xh, th_)
                        fill(last, (w, n, b))
                before = n
            for b in range(4):
                use(("UW", b))
                taken(pe, ("MX", 32, b))
                taken(pe, ("KV", b // 2))
                for h in range(4):
                    last = mm(B(("UW", b))[:, h * P:(h + 1) * P], Mm[:, 4 * b + h, :], KA[:, 4 * b + h, :])
                fill(last, ("UW", b))
            for b in range(4):
                use(("rhat", b))
                taken(pe, ("UW", b))
                for h in range(4):
                    last = mm(B(("rhat", b), DH)[:, h * P:(h + 1) * P], UW[:, 4 * b + h, DH:P], Rb[:, 4 * b + h, :])
                fill(last, ("rhat", b))
            for w, c in (("Q", 0), ("Q", 1), ("PT", 1), ("Q", 2), ("PT", 2)):
                t, lanes = c // 2, slice(DH * (c % 2), DH * (c % 2) + DH)
                use((w, c))
                for h in range(NH):
                    o = B((w, c), DH)[:, h * DH:(h + 1) * DH]
                    uw, b_, k_, v_ = (UW[lanes, t * NH + h, :], tok["b"][lanes, t, h, :], tok["k"][lanes, t, h, :],
                                      tok["v"][lanes, t, h, :])
                    if w == "Q":
                        mm(o, b_, uw[:, 0:DH], True, False)
                        last = mm(o, k_, v_, False, True)
                    else:
                        last = mm(o, uw[:, DH:P], b_)
                fill(last, (w, c))
            for c in (1, 2):
                use(("state", c))
                taken(pe, ("PT", c))
                pe.wait_ge(s["state_done"], c)
                for h in range(NH):
                    last = mm(B(("state", c), DH)[:, h * DH:(h + 1) * DH], PT[:, c, h, :], Ss[:, c - 1, h, :])
                fill(last, ("state", c))
            pe.wait_ge(s["state_done"], 3)
            for b in range(4):
                taken(pe, ("rhat", b))
            for t in range(TT):
                use(("Y", t))
                for h in range(NH):
                    j, hh = divmod(h, 2)
                    lanes = slice(DH * hh, DH * hh + DH)
                    o = psum[lanes, BANK[("Y", t)][0], j * P:(j + 1) * P]
                    mm(o, tok["v"][:, t, h, :], Rk[:, t * NH + h, :], True, False)
                    mm(o, UW[:, t * NH + h, 0:DH], Rb[:, t * NH + h, :], False, False)
                    for half in range(2):
                        c = 2 * t + half
                        if c:
                            last = mm(o[:, half * CH:(half + 1) * CH], Ss[:, c - 1, h, :],
                                      til["r"][:, h, c * CH:(c + 1) * CH], False, True)
                fill(last, ("Y", t))
            for t in range(TT):
                taken(pe, ("Y", t))
            for w, src in (("mean", yb), ("var", yq)):
                if w == "var":
                    pe.wait_ge(s["y_sq"], 1)
                flat = src.rearrange("p j s -> p (j s)")
                for q in range(2):
                    use((w, q))
                    fill(mm(B((w, q)), C("heads"), flat[:, q * 512:(q + 1) * 512]), (w, q))

            for n in range(6):
                channel_major([(c, ("merge", 4 * n + c)) for c in (0, 2)], f"merge{n}")
            for n, src in enumerate((oaT, obT, omT)):
                if n == 0:
                    taken(pe, ("oaT", 1))
                if n == 1:
                    pe.wait_ge(s["ob_done"], 1)
                w = weights(f"branch{n}").rearrange("p (c n) -> p c n", c=4)
                for ct in range(0, KD, 2):
                    job = ("branch", n, ct)
                    use(job)
                    for c in range(2):
                        for k in range(4):
                            last = mm(B(job)[:, c * S:(c + 1) * S], w[:, k, (ct + c) * P:(ct + c + 1) * P],
                                      src[:, k, :], k == 0, k == 3)
                    fill(last, job)
            pe.wait_ge(s["mix_done"], 8)
            w = [weights(f"out{n}").rearrange("p (c n) -> p c n", c=4) for n in range(2)]
            for t in range(TT):
                for q in range(2):
                    job = ("out", t, q)
                    use(job)
                    for k in range(KD):
                        last = mm(B(job), mixT[:, k, t * P:(t + 1) * P], w[k // 4][:, k % 4, q * 512:(q + 1) * 512],
                                  k == 0, k == KD - 1)
                    fill(last, job)
            for t in range(TT):
                pe.wait_ge(s["xn2_done"], t + 1)
                for q in range(2):
                    job = ("h2T", q, t)
                    use(job)
                    for k in range(4):
                        last = turn(B(job)[:, k * P:(k + 1) * P], xn2[:, t, (4 * q + k) * P:(4 * q + k + 1) * P])
                    fill(last, job)
            use(("logits",))
            for t in range(TT):
                for q in range(2):
                    taken(pe, ("h2T", q, t))
            for t in range(TT):
                o = B(("logits",))[:, t * NE:(t + 1) * NE]
                for k in range(KD):
                    mm(o, h2T[:, k, t * P:(t + 1) * P], router_w[:, k, :], k == 0, False)
                last = mm(o, C("ones")[0:1, :], router_b[0:1, :], False, True)
            fill(last, ("logits",))
            use(("rank",))
            pe.wait_ge(s["sel_done"], 1)
            o = B(("rank",))
            mm(o[:, 0:NE], C("before"), sel[:, 0, :])
            mm(o[:, NE:2 * NE], C("ones"), sel[:, 0, :], True, False)
            mm(o[:, NE:2 * NE], C("before"), sel[:, 1, :], False, True)
            mm(o[:, 2 * NE:3 * NE], C("ones"), sel[:, 0, :], True, False)
            fill(mm(o[:, 2 * NE:3 * NE], C("ones"), sel[:, 1, :], False, True), ("rank",))
            use(("gateT",))
            for t in range(TT):
                last = turn(B(("gateT",), NE)[:, t * P:(t + 1) * P], gat[:, t, :])
            fill(last, ("gateT",))
            for b in range(NB):
                pe.wait_ge(bank_free[b], LAST_USE[b])
            for t in range(TT):
                for h in range(2):
                    mm(psum[:, 2 * t + h, :], gT[0:NE, t * P:(t + 1) * P], b2_sb[0:NE, h * 512:(h + 1) * 512],
                       True, False)

            def gather():
                for d in range(KD):
                    for t in range(TT):
                        last = mm(psum[:, 4 + d // 4, d % 4 * P:(d % 4 + 1) * P], xn2[:, t, d * P:(d + 1) * P],
                                  Pk[:, t].rearrange("p k n -> p (k n)"), t == 0, t == TT - 1)
                last.then_inc(s["g_full"], 1)

            def scatter(k):
                for t in range(TT):
                    for h in range(2):
                        last = mm(psum[:, 2 * t + h, :], pgt[:, k, t * P:(t + 1) * P],
                                  osb[:, h * 512:(h + 1) * 512], False, False)
                return last

            rounds = load_rounds(pe)
            pe.wait_ge(s["P_ready"], 1)
            gather()
            with pe.Fori(0, rounds) as r:
                with pe.Fori(0, NE // 2) as i:
                    it = r * (NE // 2) + i
                    for k in range(2):
                        E = it * 2 + k

                        def up(q):
                            pe.wait_ge(moe_in[q], E * 16 + 16)
                            pe.wait_ge(s["h_out"], E * 4 + (q + 1))
                            w = slots2[q].rearrange("p (k n) -> p k n", k=KD)
                            for d in range(KD):
                                half = d % 2
                                last = mm(psum[CAP * half:CAP * half + CAP, 6 + q % 2, :],
                                          xg[:, d, CAP * k:CAP * k + CAP], w[:, d, :], d < 2, d >= KD - 2)
                            last.then_inc(s["h_full"], 1)

                        def turn_up(q):
                            pe.wait_ge(s["h_out"], E * 4 + (q + 3))
                            pe.wait_ge(s["t_out"], E * 5 + (q + 2))
                            for c in range(4):
                                last = mm(psum[:, 5, c * CAP:(c + 1) * CAP], hraw[:, q % 2, c * P:(c + 1) * P],
                                          C("twice"))
                            last.then_inc(s["t_full"], 1)

                        if k == 0:
                            pe.wait_ge(s["xg_ready"], it + 1)
                        up(0)
                        pe.wait_ge(s["o_free"], E + 1)
                        pe.wait_ge(s["pg_ready"], E + 1)
                        pe.wait_ge(s["t_out"], E * 5 + 1)
                        for t in range(TT):
                            last = turn(psum[:, 5, t * P:(t + 1) * P], PG[:, t].rearrange("p k n -> p (k n)"))
                        last.then_inc(s["t_full"], 1)
                        up(1)
                        turn_up(0)
                        up(2)
                        turn_up(1)
                        up(3)
                        turn_up(2)
                        turn_up(3)
                        pe.wait_ge(s["t_out"], E * 5 + 6)
                        if k == 1:
                            pe.wait_ge(s["P_ready"], it + 2)
                            gather()
                        scatter(1 - k)
                        pe.wait_ge(s["a_ready"], E * 4 + 4)
                        if k == 1:
                            pe.wait_ge(s["xg_ready"], it + 2)
                        for part in range(2):
                            pe.wait_ge(moe_in[4 + part], E * 16 + 16)
                            w = slots2[4 + part].rearrange("p (c n) -> p c n", c=4)
                            for h in range(2):
                                for c in range(4):
                                    half = c % 2
                                    last = mm(psum[CAP * half:CAP * half + CAP, 4 + h, :], act[:, 4 * part + c, :],
                                              w[:, c, h * 512:(h + 1) * 512], part == 0 and c < 2,
                                              part == 1 and c >= 2)
                            last.then_inc(s["o_full"] if part else s["o_half"], 1)
            pe.wait_ge(s["o_free"], rounds * NE + 1)
            scatter(1).then_inc(s["y_full"], 1)


def kernel(x, mem, g_mix, g_mem, w_in, b_merge, nsa_q_norm, nsa_k_norm, cmp_pe, cmp_w1, cmp_b1, cmp_w2,
           rwkv_shift_mix, rwkv_w0, rwkv_w_up, rwkv_a0, rwkv_a_up, rwkv_g_up, rwkv_k_k, rwkv_k_a, rwkv_r_k,
           rwkv_ln_w, rwkv_ln_b, mem_w_kv, mem_q_norm, mem_k_norm, w_branch, w_out, g_ffn,
           router_w, router_b, exp_w1, exp_b1, exp_w2, exp_b2):
    from concourse import bacc
    from concourse.bass_utils import run_bass_kernel_spmd

    def rows(w):
        w = np.asarray(w)
        return np.ascontiguousarray(w.reshape(-1, P, w.shape[-1]).transpose(1, 0, 2))

    w_in = np.asarray(w_in)[0]
    at, parts = 0, {}
    for name, n in (("q", 512), ("kcmp", 128), ("vcmp", 128), ("kslc", 128), ("vslc", 128), ("kwin", 128),
                    ("vwin", 128), ("gate", 24), ("shift", 1792), ("qm", 512), ("merge", 3072)):
        parts[name] = w_in[:, at:at + n]
        at += n
    kv = np.asarray(mem_w_kv)[0]
    blocks = [parts["shift"][:, n * 512:(n + 1) * 512] for n in range(4)]
    blocks += [parts["q"], np.concatenate([parts[n] for n in ("kslc", "kwin", "kcmp", "vcmp")], 1),
               np.concatenate([parts[n] for n in ("vslc", "vwin", "gate")], 1), parts["qm"], kv[:, :512], kv[:, 512:]]
    merge = [parts["merge"][:, n * 512:(n + 1) * 512] for n in range(6)]
    weights = np.zeros((len(W1_UNITS), P, UNIT), np.float32)

    def put(name, w):
        weights[W1_AT[name]].reshape(P, w.shape[1], -1)[:, :, :w.shape[2]] = w

    for name, w in zip(W1_UNITS[:10], blocks):
        put(name, rows(w))
    weights[W1_AT["cmp1"]] = np.asarray(cmp_w1)[0].reshape(2, 16, P, P).transpose(2, 0, 1, 3).reshape(P, UNIT)
    for n, w in enumerate(merge):
        put(f"merge{n}", rows(w))
    for n in range(3):
        put(f"branch{n}", rows(np.asarray(w_branch)[0, n]))
    for n in range(2):
        put(f"out{n}", rows(np.asarray(w_out)[0, n * 512:(n + 1) * 512]))

    vec = np.zeros((P, NVEC), np.float32)
    for name, a in (("g_mix", g_mix), ("g_mem", g_mem), ("g_ffn", g_ffn), ("b_merge", b_merge),
                    ("mix", rwkv_shift_mix), ("w0", rwkv_w0), ("a0", rwkv_a0), ("k_k", rwkv_k_k), ("k_a", rwkv_k_a),
                    ("r_k", rwkv_r_k), ("ln_w", rwkv_ln_w), ("ln_b", rwkv_ln_b), ("cmp_b1", cmp_b1),
                    ("mq_n", mem_q_norm), ("mk_n", mem_k_norm)):
        o, n = VEC[name]
        vec[:, o:o + n] = np.asarray(a).reshape(n, P).T

    w1 = np.asarray(exp_w1)[0].reshape(NE, KD, P, 4, 256, 2)
    experts = np.empty((NE, N2, P, UNIT), np.float32)
    experts[:, 0:4].reshape(NE, 4, P, KD, 2, 256)[...] = w1.transpose(0, 3, 2, 1, 5, 4)
    experts[:, 4:6].reshape(NE, 2, P, 4, D)[...] = np.asarray(exp_w2)[0].reshape(NE, 2, 4, P, D).transpose(0, 1, 3, 2, 4)
    b1 = np.asarray(exp_b1)[0].reshape(NE, 4, 2, P, 2).transpose(3, 0, 1, 4, 2)
    q_n, k_n = np.asarray(nsa_q_norm)[0], np.asarray(nsa_k_norm)[0]
    arrays = {
        "x": np.asarray(x), "mem": np.asarray(mem), "weights": weights, "const": shape_constants(), "vec": vec,
        "experts": experts, "exp_b1": np.ascontiguousarray(b1).reshape(P, NE * 16),
        "exp_b2": np.asarray(exp_b2)[0],
        "up": np.concatenate([np.concatenate([np.asarray(rwkv_w_up)[0], np.asarray(rwkv_a_up)[0]], 0),
                              np.asarray(rwkv_g_up)[0]], 1),
        "cmp_w2": np.ascontiguousarray(np.asarray(cmp_w2)[0].transpose(1, 0, 2)).reshape(P, 2 * DH),
        "cmp_pe": np.ascontiguousarray(np.asarray(cmp_pe)[0].reshape(2, 16, P).transpose(2, 0, 1)).reshape(P, 32),
        "head_norms": np.concatenate([q_n] * 8 + [k_n[1]] * 2 + [k_n[2]] * 2)[None],
        "cmp_norm": k_n[0][None],
        "router_w": rows(np.asarray(router_w)[0]).reshape(P, KD * NE), "router_b": np.asarray(router_b),
    }
    nc = bacc.Bacc("TRN2", target_bir_lowering=False, num_devices=1)
    ins = {}
    for name, arr in arrays.items():
        arr = arrays[name] = np.ascontiguousarray(arr)
        ins[name] = nc.dram_tensor(name, arr.shape, F32, kind="ExternalInput").ap()
    out = nc.dram_tensor("out", (1, S, D), F32, kind="ExternalOutput").ap()
    build(nc, ins, out)
    r = run_bass_kernel_spmd(nc, [arrays], core_ids=[0])
    return r.results[0]["out"]
```

```python
from contextlib import ExitStack

import numpy as np

import concourse.bass as bass
from concourse import mybir

ALU = mybir.AluOpType
ACT = mybir.ActivationFunctionType
AX = mybir.AxisListType
F32 = mybir.dt.float32
U32 = mybir.dt.uint32
I32 = mybir.dt.int32

P = 128
D = 1024
S = 256
TT = S // P
KD = D // P
DH = 64
NH = 8
NG = 2
CMP_L, CMP_ST = 32, 16
NC = (S - CMP_L) // CMP_ST + 1
CH = 64
NCH = S // CH
MH, MD = 4, 128
NE, TOPK = 32, 4
CAP = 64
ROUNDS = -(-S // CAP)
NEG = -1.0e30
EPS = 1e-6
GN_EPS = 64e-5
EM05 = float(np.exp(-0.5))
UNIT = 4096
N1 = 2
UNITS2 = 6
W2_AT = 4
TWICE = (0, 4, 5)

VEC = {}
for _name, _n in (("g_mix", 8), ("g_mem", 8), ("g_ffn", 8), ("b_merge", 24), ("mix", 14), ("w0", 4), ("a0", 4),
                  ("k_k", 4), ("k_a", 4), ("r_k", 4), ("ln_w", 4), ("ln_b", 4), ("cmp_b1", 2),
                  ("mq_n", 1), ("mk_n", 1)):
    VEC[_name] = (sum(n for _, n in VEC.values()), _n)
NVEC = sum(n for _, n in VEC.values())

CONST = {}
for _name, _n in (("ident", P), ("half", 32), ("low", P), ("upp", P), ("uppi", P), ("heads", P), ("before", P), ("ones", P),
                  ("up2", P), ("up4", P), ("up8", P), ("up16", P), ("up32", P),
                  ("lo1", P),
                  ("causal", 2 * P), ("cmpneg", 2 * NC), ("cmpok", 2 * NC), ("cos", 2 * DH), ("sin", 2 * DH),
                  ("twice", CAP), ("ccos", DH), ("csin", DH), ("slots", CAP), ("experts", NE), ("gn_eps", 1)):
    CONST[_name] = (sum(n for _, n in CONST.values()), _n)
NCONST = sum(n for _, n in CONST.values())
EARLY = P + 32


def shape_constants():
    c = np.zeros((P, NCONST), np.float32)

    def put(name, a):
        o, n = CONST[name]
        c[:a.shape[0], o:o + n] = a.reshape(a.shape[0], n)

    i, j = np.arange(P)[:, None], np.arange(P)[None, :]
    chunk = i // CH == j // CH
    put("ident", (i == j) * 1.0)
    put("low", (i > j) * chunk * 1.0)
    put("upp", (i < j) * chunk * 1.0)
    put("uppi", (i <= j) * chunk * 1.0)
    put("heads", (i // DH == j // DH) * 1.0)
    put("before", (i < j) * 1.0)
    put("ones", np.ones((P, P)))
    for n in (1, 2, 4, 8, 16, 32):
        off = (i // (2 * n) == j // (2 * n)) & (i // n % 2 == 0) & (j // n % 2 == 1)
        if n == 1:
            put("lo1", off.T * 1.0)
        else:
            put(f"up{n}", off * 1.0)
    put("causal", np.concatenate([np.zeros((P, P)), np.where(j <= i, 0.0, NEG)], 1))
    pos = np.arange(P)[:, None, None] + P * np.arange(TT)[None, :, None]
    end = np.arange(NC)[None, None, :] * CMP_ST + CMP_L - 1
    put("cmpneg", np.where(end <= pos, 0.0, NEG))
    put("cmpok", (end <= pos) * 1.0)
    inv = np.float32(10000.0) ** (-np.arange(0, DH, 2, dtype=np.float32) / np.float32(DH))

    def rope(at):
        ang = at.astype(np.float32)[..., None] * inv
        cos, sin = np.cos(ang), np.sin(ang)
        return np.concatenate([cos, cos], -1), np.concatenate([-sin, sin], -1)

    cos, sin = rope(pos[..., 0])
    put("cos", cos)
    put("twice", (i[:, 0:1] % CAP == np.arange(CAP)) * 1.0)
    put("sin", sin)
    cos, sin = rope(np.arange(NC) * CMP_ST + CMP_L - 1)
    put("ccos", cos)
    put("csin", sin)
    put("slots", np.tile(np.arange(CAP), (P, 1)))
    put("experts", np.tile(np.arange(NE), (P, 1)))
    put("gn_eps", np.full((P, 1), GN_EPS))
    put("half", np.full((P, 32), -0.5))
    return c


UNITS = ([("cmp", g, t, 4, 0) for t in range(TT) for g in range(NG)]
         + [(kind, g * 4 + h, t, 4 if t == 0 else 2, t + 1) for kind in ("slc", "win") for g in range(NG)
            for t in range(TT) for h in ((0,) if t == 0 else (0, 2))]
         + [("mem", h, t, 2, 2) for t in range(TT) for h in (0, 2)])
LEVELS = (2, 4, 8, 16, 32)
MERGE_T = 3 * KD
MERGE_CUTS = {"attention": 5, "ksum": 5, "state": 1, "Y": 1}
LATE_SHIFTS = (6, 8, 10, 12)
FILL_UNITS = [u for u in range(len(UNITS)) if u < len(UNITS) - 2]
BRANCHES = (0, 2, 1)
MERGES, _at = {}, 0
for _name, _n in MERGE_CUTS.items():
    MERGES[_name] = [2 * (_at + i) for i in range(_n)]
    _at += _n
assert 2 * _at == MERGE_T
FILL = [("shift", ct) for ct in LATE_SHIFTS] + [("merge", ct) for ct in MERGES["attention"]]
assert len(FILL_UNITS) == 2 * len(FILL)


def attention_jobs():
    jobs = [("scores", 0), ("scores", 1)]
    for u in range(len(UNITS)):
        jobs += [("turn", u)] + ([("scores", u + 2)] if u + 2 < len(UNITS) else [])
        jobs.append(("values", u))
        if u in FILL_UNITS[::2]:
            jobs.append(FILL[FILL_UNITS.index(u) // 2])
    return jobs


def merge_jobs(where):
    return [("merge", ct) for ct in MERGES[where]]


def inverse_jobs():
    jobs = []
    for n in LEVELS:
        jobs += [("X", n, b) for b in range(4)]
        jobs += [("TT", n, b) for b in range(4) if n > 2]
        jobs += [("MX", n, b) for b in range(4)]
    return jobs


JOBS = ([("hT", q, t) for t in range(TT) for q in range(2)] + [("q", t) for t in range(TT)]
        + [("mT", q, t) for t in range(TT) for q in range(2)] + [("kc", t) for t in range(TT)]
        + [(w, t) for w in ("vg", "qm") for t in range(TT)] + [("kcT",)]
        + [(w, t) for w in ("km", "vm") for t in range(TT)]
        + [("hid",), ("shift", 0), ("shift", 2), ("cmp2",), ("shift", 4), ("cT",)]
        + [("qkT", t, q) for t in range(TT) for q in range(3)]
        + [("memT", w, t) for w in "qk" for t in range(TT)]
        + attention_jobs()
        + [("oaT", t) for t in range(TT)] + [("omT", t) for t in range(TT)]
        + [("up", w, q) for w in "wag" for q in range(2)]
        + [("ksum", q) for q in range(2)] + merge_jobs("ksum") + [("bonus", q) for q in range(2)]
        + [("vtok", t) for t in range(TT)]
        + [("tok", w, t) for w in "akb" for t in range(TT)]
        + [("A", b) for b in range(4)]
        + [(w, b) for w in ("Kk", "Rb", "Rk") for b in range(4)]
        + [("M1", b) for b in range(4)]
        + [("KV", t) for t in range(TT)]
        + inverse_jobs()
        + [("UW", b) for b in range(4)] + [("rhat", b) for b in range(4)]
        + [("Q", 0), ("Q", 1), ("PT", 1), ("Q", 2), ("PT", 2)]
        + merge_jobs("state") + [("state", 1), ("state", 2)]
        + [("Y", t) for t in range(TT)] + merge_jobs("Y")
        + [("mean", q) for q in range(2)] + [("var", q) for q in range(2)]
        + [("branch", n, ct) for n in BRANCHES for ct in range(0, KD, 2)]
        + [("out", 0, 0), ("out", 0, 1), ("out", 1, 0), ("h2T", 0, 0), ("h2T", 1, 0), ("out", 1, 1)]
        + [("logits", 0), ("h2T", 0, 1), ("h2T", 1, 1), ("logits", 1), ("rank",), ("gateT",)])
NB = 8
BANK = {job: (n % NB, n // NB) for n, job in enumerate(JOBS)}
LAST_USE = [max(BANK[j][1] for j in JOBS if BANK[j][0] == b) + 1 for b in range(NB)]

W1_UNITS = (["q", "kc", "vg", "qm", "km", "vm", "cmp1", "shift0", "shift1", "shift2", "shift3"]
            + [f"merge{n}" for n in range(6)] + [f"branch{n}" for n in BRANCHES] + ["out0", "out1"])
W1_AT = {name: n for n, name in enumerate(W1_UNITS)}

SEMS = """mem_in const_in tables_in small_in out_in late_in x_out
 v_step a_step xsq_done xr_done xn_done pp_done wa_done xg_done
 qk_sq qk_ss qk_r qk_rot R_zero tanh_in tanh_out ge_done kc_sq kc_r kc_rot
 qm_sq qm_r qm_n gate_raw m_ready e_ready cmp_ok values_done
 decay_done k_sq rk_done tilde_done lg_ss lg_exp
 state_done y_sq ob_done mix_done router_ready zeros_done x1_sq x1_r xn2_done sel_done gat_done scratch_free
 P_ready pg_ready g_full xg_ready h_full h_out t_full t_out x_ready t_ready a_ready o_half o_full o_free v2_step
 y_full y_out""".split()


class Arena:

    def __init__(self, tensor, size):
        self.tensor, self.size, self.at = tensor, size, 0

    def take(self, *dims, parts=P):
        n = int(np.prod(dims))
        assert self.at + n <= self.size, (self.at, n)
        v = self.tensor[0:parts, self.at:self.at + n]
        self.at += n
        if len(dims) == 2:
            v = v.rearrange("p (a b) -> p a b", a=dims[0])
        elif len(dims) == 3:
            v = v.rearrange("p (a b c) -> p a b c", a=dims[0], b=dims[1])
        elif len(dims) == 4:
            v = v.rearrange("p (a b c d) -> p a b c d", a=dims[0], b=dims[1], c=dims[2])
        return v


class Steps:

    def __init__(self, eng, own, bank_free, bank_full):
        self.eng, self.own, self.bank_free, self.bank_full = eng, own, bank_free, bank_full
        self.counts, self.last = {}, None

    def do(self, ins, sem=None):
        sem = sem or self.own
        self.counts[sem.name] = self.counts.get(sem.name, 0) + 1
        ins.then_inc(sem, 1)
        self.last = (sem, self.counts[sem.name])

    def free(self, ins, job):
        b, used = BANK[job]
        ins.then_inc(self.bank_free[b], 1)
        self.last = (self.bank_free[b], used + 1)

    def full(self, job):
        b, used = BANK[job]
        self.eng.wait_ge(self.bank_full[b], used + 1)

    def settle(self):
        self.eng.wait_ge(*self.last)


def bc(ap, axis, n):
    v = ap.unsqueeze(axis)
    shape = list(v.shape)
    shape[axis] = n
    return v.to_broadcast(shape)


def build(nc, ins, out):
    with ExitStack() as ctx:
        arena_size = (nc.sbuf_bytes_remaining - 256) // 4
        arena = Arena(ctx.enter_context(nc.sbuf_tensor("arena", [P, arena_size], F32)), arena_size)
        psum = ctx.enter_context(nc.psum_tensor("banks", [P, NB, 512], F32))
        s = {n: ctx.enter_context(nc.semaphore(n)) for n in SEMS}
        bank_full = [ctx.enter_context(nc.semaphore(f"bank_full{b}")) for b in range(NB)]
        bank_free = [ctx.enter_context(nc.semaphore(f"bank_free{b}")) for b in range(NB)]
        unit_in = [ctx.enter_context(nc.semaphore(f"weights_in{b}")) for b in range(N1)]
        x_in = [ctx.enter_context(nc.semaphore(f"x_in{t}")) for t in range(TT)]
        expert_in = []
        for j in range(UNITS2):
            if j in TWICE:
                expert_in.append([ctx.enter_context(nc.semaphore(f"unit{j}_{w}_in")) for w in ("even", "odd")])
            else:
                expert_in.append([ctx.enter_context(nc.semaphore(f"unit{j}_in"))] * 2)
        A = arena
        slots = [A.take(UNIT) for _ in range(N1)]
        const = A.take(NCONST)
        vec = A.take(NVEC)

        def C(name, *dims, parts=P):
            o, n = CONST[name]
            v = const[0:parts, o:o + n]
            return v.rearrange("p (a b) -> p a b", a=dims[0]) if dims else v

        def V(name, i=None):
            o, n = VEC[name]
            return vec[:, o:o + n] if i is None else vec[:, o + i:o + i + 1]

        ident = C("ident")
        hw0, ha0, hbm, omka = A.take(4), A.take(4), A.take(24), A.take(4)
        router_w = A.take(KD, NE)
        router_b = A.take(NE)
        b2_sb = A.take(D)
        stat = A.take(8)
        rstd = A.take(8)
        hT_at = A.at
        hT = A.take(KD, S)
        oaT, omT = A.take(4, S), A.take(4, S)
        inner = A.at
        up_w, up_g = A.take(512), A.take(512)
        obT = A.take(4, S)
        region = A.at

        xs, ms = A.take(TT, D), A.take(TT, D)
        mT = A.take(KD, S)
        pbuf = A.take(14, S + 1)
        qk = A.take(TT, 12, DH)
        kcv = A.take(TT, 2, P)
        vg = A.take(TT, 280)
        qm, km, vm = A.take(TT, MH, MD), A.take(TT, MH, MD), A.take(TT, MH, MD)
        qkT = A.take(12, S, parts=DH)
        R = A.take(2, 16, 31)
        mT4 = mT.rearrange("p (w h) s -> p w h s", w=2)
        qmT, kmT = mT4[:, 0], mT4[:, 1]
        cw2, pe_sb = A.take(2, DH), A.take(2, 16)
        nwt = A.take(12, DH)
        kn0 = A.take(DH, parts=NC)
        rs, rr = A.take(24), A.take(24)
        rsm, rrm = A.take(16), A.take(16)
        gates = A.take(TT, NH * 3)
        hbias, hx, hu, ge = A.take(2), A.take(2, 30), A.take(2, 30), A.take(2, 30)
        ctok, csq, crot = A.take(2, 2, DH, parts=NC), A.take(2, DH, parts=NC), A.take(2, DH, parts=NC)
        cs2, cr2 = A.take(2, parts=NC), A.take(2, parts=NC)
        kcT = A.take(2, NC, parts=DH)
        osum, omem = A.take(TT, NH, DH), A.take(TT, MH, MD)
        shared = A.at
        rot1, rot2 = A.take(TT, 12, DH), A.take(TT, 12, DH)
        sqx = rot1.rearrange("p a b c -> p (a b c)")[:, 0:D]
        A.at = shared
        sb_s, sb_e, sb_eT = A.take(2, 512), A.take(2, 512), A.take(2, 512)
        mx, nmx, sm, fac = A.take(2, 4), A.take(2, 4), A.take(2, 4), A.take(2, 4)
        otmp = A.take(2, 256)
        tg_at = arena_size - MERGE_T * S
        tg = arena.tensor[:, tg_at:arena_size].rearrange("p (c s) -> p c s", c=MERGE_T)
        assert A.at <= tg_at, (A.at, tg_at)

        A.at = region
        pp = A.take(14, S)
        A.at = region
        Rb, Rk = A.take(16, P), A.take(16, P)
        til = {w: A.take(NH, S, parts=DH) for w in "abkr"}
        gg, bon = A.take(4, S), A.take(4, S)
        DC = A.take(NH, NCH, parts=DH)
        tok = {w: A.take(TT, NH, DH) for w in "vkb"}
        KA = A.take(16, P)
        scratch = A.at
        dE, Dc = A.take(16, CH + 1), A.take(16, CH + 1)
        Di, aa, kkn, tmp = A.take(4, S), A.take(4, S), A.take(4, S), A.take(4, S)
        pat = A.take(16 * (CH + 1))
        A.at = scratch
        Mm = A.take(16, P)
        Am, Tm = A.take(16, P), A.take(16, P)
        UW = A.take(16, P)
        assert A.at <= tg_at, (A.at, tg_at)
        Kk = UW
        A.at = scratch
        yb = A.take(4, S)
        yq = A.take(4, S)
        PT, Qs = A.take(3, NH, DH, parts=DH), A.take(3, NH, DH, parts=DH)
        assert A.at <= scratch + 6144
        A.at = inner
        Xm = A.take(4, 512)
        assert A.at <= region
        A.at = inner
        Ss = A.take(3, NH, DH, parts=DH)
        stmp = A.take(NH, DH, parts=DH)
        assert A.at <= region

        A.at = inner + UNIT
        x1 = A.take(TT, D)
        xn2 = A.take(TT, D)
        rankR, gateR = A.take(TT, ROUNDS * NE + 2), A.take(TT, ROUNDS * NE + 2)
        b1_sb = A.take(NE, 16)
        Pk, PG = A.take(TT, 2, CAP), A.take(TT, 2, CAP)
        xg, act = A.take(KD, 2 * CAP), A.take(KD, CAP)
        hraw = A.take(2, 512)
        hb, xlo, xhi, th = A.take(2, 4 * CAP), A.take(2, 2 * CAP), A.take(2, 2 * CAP), A.take(2, 2 * CAP)
        osb = A.take(D)
        pgt = A.take(2, S)
        nrounds = A.take(1).bitcast(I32)
        nz = A.take(2)
        mixT_at = A.at
        mixT = A.take(KD, S)
        moe_top = arena_size - (UNITS2 - N1) * UNIT
        h2T = A.take(KD, S)
        lg, sel, gat = A.take(TT, NE), A.take(TT, NE), A.take(TT, NE)
        top, idx, idf = A.take(TT, 8), A.take(TT, 8).bitcast(U32), A.take(TT, 8)
        et, es, er = A.take(TT, 4), A.take(TT), A.take(TT)
        rk1 = A.take(TT, NE)
        chosen = A.take(TT, TOPK, NE)
        cm = A.take(8)
        mprod = hraw
        gT = A.take(S)
        assert A.at <= moe_top, (A.at, moe_top)

        def slot_at(at):
            return arena.tensor[:, at:at + UNIT]

        tops = [slot_at(moe_top + i * UNIT) for i in range(UNITS2 - N1)]
        w1_slots = [[slots[0], slot_at(inner)]] + [[w, w] for w in (slots[1], tops[0], tops[1])]
        w2_slots = [[tops[2], slot_at(hT_at)], [tops[3], slot_at(mixT_at)]]
        out_w = tops[0:2]

        def B(job, parts=P):
            return psum[0:parts, BANK[job][0], :]

        def taken(eng, job):
            b, used = BANK[job]
            eng.wait_ge(bank_free[b], used + 1)

        def filled(eng, job):
            b, used = BANK[job]
            eng.wait_ge(bank_full[b], used + 1)

        def load_rounds(eng):
            eng.wait_ge(s["scratch_free"], 1)
            return eng.value_load(nrounds[0:1, 0:1], min_val=1, max_val=ROUNDS)

        block = ctx.enter_context(nc.Block())

        @block.sync
        def _(sp):
            rows = "b (t p) d -> p (b t) d"
            for t in range(TT):
                sp.dma_start(xs[:, t, :], ins["x"].rearrange(rows, p=P)[:, t]).then_inc(x_in[t], 16)
                if t == 0:
                    sp.dma_start(const[:, 0:EARLY], ins["const"][:, 0:EARLY]).then_inc(s["const_in"], 16)
                    sp.dma_start(vec, ins["vec"]).then_inc(s["const_in"], 16)
            last = {"shift0": ("shift", 2), "shift1": ("shift", 6), "shift2": ("shift", 10), "shift3": ("shift", 12),
                    "cmp1": ("hid",), "branch0": ("branch", 0, 6), "branch1": ("branch", 1, 6),
                    "branch2": ("branch", 2, 6)}
            last |= {w: (w, 1) for w in ("q", "kc", "vg", "qm", "km", "vm")}
            last |= {f"merge{n}": ("merge", 4 * n + 2) for n in range(6)}
            for n, name in enumerate(W1_UNITS[:-2]):
                if n >= N1:
                    filled(sp, last[W1_UNITS[n - N1]])
                sp.dma_start(slots[n % N1], ins["weights"][n]).then_inc(unit_in[n % N1], 16)
                if n == 0:
                    sp.dma_start(const[:, EARLY:], ins["const"][:, EARLY:]).then_inc(s["tables_in"], 16)
                    sp.dma_start(ms, ins["mem"].rearrange(rows, p=P)).then_inc(s["mem_in"], 16)
                if n == N1 - 1:
                    for dst, src in ((up_w, ins["up"][:, 0:512]), (up_g, ins["up"][:, 512:1024]),
                                     (cw2.rearrange("p a b -> p (a b)"), ins["cmp_w2"]),
                                     (nwt.rearrange("p a b -> p (a b)"), ins["head_norms"].partition_broadcast(P)),
                                     (kn0, ins["cmp_norm"].partition_broadcast(NC)),
                                     (pe_sb.rearrange("p a b -> p (a b)"), ins["cmp_pe"]),
                                     (router_w.rearrange("p a b -> p (a b)"), ins["router_w"]),
                                     (router_b[0:1], ins["router_b"]), (b2_sb[0:NE], ins["exp_b2"])):
                        sp.dma_start(dst, src).then_inc(s["small_in"], 16)
            sp.wait_ge(s["ob_done"], 1)
            for n in range(2):
                sp.dma_start(out_w[n], ins["weights"][W1_AT[f"out{n}"]]).then_inc(s["out_in"], 16)
            sp.dma_start(x1, ins["x"].rearrange(rows, p=P)).then_inc(s["late_in"], 16)
            sp.dma_start(b1_sb.rearrange("p a b -> p (a b)"), ins["exp_b1"]).then_inc(s["late_in"], 16)
            def load(k, e, j):
                dst = w1_slots[j][k] if j < W2_AT else w2_slots[j - W2_AT][k]
                sp.dma_start(dst, ins["experts"][bass.ds(e, 1), j].rearrange("e p n -> (e p) n")
                             ).then_inc(expert_in[j][k], 16)

            def reload(k, E, e, units):
                for j in units:
                    if j == 0:
                        sp.wait_ge(s["h_full"], E * 4 - 7)
                    elif j < W2_AT:
                        sp.wait_ge(s["h_full"], E * 4 + (j - 3))
                    else:
                        sp.wait_ge(s["o_half"] if j == W2_AT else s["o_full"], E - 1)
                    load(k, e, j)

            filled(sp, ("branch", BRANCHES[-1], KD - 2))
            load(0, 0, 0)
            load(0, 0, 1)
            load(1, 1, 0)
            sp.wait_ge(s["mix_done"], 8)
            for j in range(W2_AT, UNITS2):
                load(0, 0, j)
            filled(sp, ("out", 1, 1))
            for j in range(N1, W2_AT):
                load(0, 0, j)
            load(1, 1, W2_AT)
            filled(sp, ("logits", 1))
            load(1, 1, W2_AT + 1)
            reload(0, 2, 2, (0,))
            reload(1, 1, 1, (1, 2, 3))
            reload(0, 2, 2, range(1, UNITS2))
            reload(1, 3, 3, range(UNITS2))
            with sp.Fori(2, NE // 2) as i:
                for k in range(2):
                    reload(k, i * 2 + k, i * 2 + k, range(UNITS2))
            rounds = load_rounds(sp)
            with sp.If(rounds > 1):
                with sp.Fori(1, rounds) as r:
                    with sp.Fori(0, NE // 2) as i:
                        for k in range(2):
                            reload(k, r * NE + i * 2 + k, i * 2 + k, range(UNITS2))
            for t in range(TT):
                sp.wait_ge(s["y_out"], t + 1)
                sp.dma_start(out.rearrange(rows, p=P)[:, t], x1[:, t, :]).then_inc(s["x_out"], 16)
            sp.wait_ge(s["x_out"], 16 * TT)

        @block.gpsimd
        def _(eng):
            def inv_sqrt(after, n, dst, src, width, sem, parts=P):
                eng.wait_ge(after, n)
                eng.tensor_tensor(dst, src, C("half", parts=parts)[:, 0:width], ALU.pow).then_inc(sem, 1)

            eng.memset(pbuf[:, :, 0:1], 0.0).then_inc(s["R_zero"], 1)
            eng.wait_ge(s["const_in"], 32)
            for i in range(2):
                inv_sqrt(s["xsq_done"], i + 1, rstd[:, 2 * i:2 * i + 2], stat[:, 2 * i:2 * i + 2], 2, s["xr_done"])
            taken(eng, ("q", 1))
            taken(eng, ("kc", 1))
            eng.tensor_tensor(rot1, qk, qk, ALU.mult).then_inc(s["qk_sq"], 1)
            inv_sqrt(s["qk_ss"], 1, rr, rs, 24, s["qk_r"])
            inv_sqrt(s["qm_sq"], 1, rrm, rsm, 16, s["qm_r"])
            inv_sqrt(s["kc_sq"], 1, cr2, cs2, 2, s["kc_r"], NC)
            eng.wait_ge(s["ob_done"], 1)
            eng.memset(osb, 0.0).then_inc(s["zeros_done"], 1)
            eng.memset(pgt, 0.0).then_inc(s["zeros_done"], 1)
            for t in range(TT):
                inv_sqrt(s["x1_sq"], t + 1, rstd[:, 4 + t:5 + t], stat[:, 4 + t:5 + t], 1, s["x1_r"])

        @block.vector
        def _(eng):
            v = Steps(eng, s["v_step"], bank_free, bank_full)
            do, free, full, settle = v.do, v.free, v.full, v.settle
            tt, ts, stt, cp = eng.tensor_tensor, eng.tensor_scalar, eng.scalar_tensor_tensor, eng.tensor_copy

            def row_max(dst, src):
                return eng.tensor_reduce(dst, src, AX.X, ALU.max)

            def row_sum(dst, src):
                return eng.tensor_reduce(dst, src, AX.X, ALU.add)

            for i, src in enumerate((xs, ms)):
                for t in range(TT):
                    eng.wait_ge(s["mem_in"] if i else x_in[t], 16)
                    do(eng.tensor_tensor_reduce(sqx, src[:, t, :], src[:, t, :], 1.0, 0.0, ALU.mult, ALU.add,
                                                stat[:, 2 * i + t:2 * i + t + 1]))
                    settle()
                both = stat[:, 2 * i:2 * i + 2]
                do(ts(both, both, 1.0 / D, EPS, ALU.mult, ALU.add), s["xsq_done"])
                if i == 0:
                    eng.wait_ge(s["const_in"], 32)
                    do(ts(hw0, V("w0"), 0.5, None, ALU.mult))
                    do(ts(ha0, V("a0"), 0.5, None, ALU.mult))
                    do(ts(hbm, V("b_merge"), 0.5, None, ALU.mult))
                    do(ts(omka, V("k_a"), -1.0, 1.0, ALU.mult, ALU.add))
                eng.wait_ge(s["xr_done"], i + 1)
                for t in range(TT):
                    do(ts(src[:, t, :], src[:, t, :], rstd[:, 2 * i + t:2 * i + t + 1], None, ALU.mult),
                       s["xn_done"])
                job, dst, gain = (("hT", hT, "g_mix"), ("mT", mT, "g_mem"))[i]
                for t in range(TT):
                    for q in range(2):
                        full((job, q, t))
                        free(tt(dst[:, 4 * q:4 * q + 4, t * P:(t + 1) * P],
                                B((job, q, t)).rearrange("p (k n) -> p k n", k=4),
                                bc(V(gain)[:, 4 * q:4 * q + 4], 2, P), ALU.mult), (job, q, t))

            def shift_mix(ct):
                taken(eng, ("shift", ct))
                do(tt(pp[:, ct:ct + 2, :], pbuf[:, ct:ct + 2, 0:S], pbuf[:, ct:ct + 2, 1:S + 1], ALU.subtract))
                settle()
                for c in (ct, ct + 1):
                    do(stt(pp[:, c, :], pp[:, c, :], V("mix", c), pbuf[:, c, 1:S + 1], ALU.mult, ALU.add),
                       s["pp_done"])

            eng.wait_ge(s["tables_in"], 16)
            eng.wait_ge(s["small_in"], 144)
            do(tt(router_w, router_w, bc(V("g_ffn"), 2, NE), ALU.mult), s["router_ready"])
            eng.wait_ge(s["qk_sq"], 1)
            do(row_sum(rs, rot1.rearrange("p t h d -> p (t h) d")))
            settle()
            do(ts(rs, rs, 1.0 / DH, EPS, ALU.mult, ALU.add), s["qk_ss"])
            eng.wait_ge(s["qk_r"], 1)
            flat = qk.rearrange("p t h d -> p (t h) d")
            do(tt(flat, flat, bc(rr, 2, DH), ALU.mult))
            settle()
            for t in range(TT):
                do(tt(qk[:, t], qk[:, t], nwt, ALU.mult))
            settle()
            half = DH // 2

            def rope(dst, src, a, b, cos, sin, heads):
                do(tt(a, src, bc(cos, 1, heads), ALU.mult))
                do(tt(b[..., 0:half], src[..., half:DH], bc(sin[:, 0:half], 1, heads), ALU.mult))
                do(tt(b[..., half:DH], src[..., 0:half], bc(sin[:, half:DH], 1, heads), ALU.mult))
                settle()

            for t in range(TT):
                rope(qk[:, t], qk[:, t], rot1[:, t], rot2[:, t], C("cos", 2)[:, t], C("sin", 2)[:, t], 12)
                do(tt(qk[:, t], rot1[:, t], rot2[:, t], ALU.add), s["qk_rot"])
            do(cp(R[:, :, :, 30], pe_sb))
            full(("kcT",))
            src = B(("kcT",)).rearrange("p (j c l two) -> p j two l c", j=2, c=16, two=2)
            n = 0
            for g in range(NG):
                for par in range(2):
                    for h in range(2):
                        for j in range(2):
                            n += 1
                            ins_ = cp(R[DH * par:DH * par + DH, j, 8 * h:8 * h + 8, g * NC:(g + 1) * NC],
                                      src[DH * g:DH * g + DH, j, par, :, h:h + NC])
                            if n == 16:
                                free(ins_, ("kcT",))
                            else:
                                do(ins_)
            taken(eng, ("km", 1))
            for i, (src, t, h) in enumerate((src, t, h) for src in (qm, km) for t in range(TT) for h in range(MH)):
                do(eng.tensor_tensor_reduce(rot2[:, 0, 0:2, :].rearrange("p a b -> p (a b)"), src[:, t, h, :],
                                            src[:, t, h, :], 1.0, 0.0, ALU.mult, ALU.add, rsm[:, i:i + 1]))
                settle()
            do(ts(rsm, rsm, 1.0 / MD, EPS, ALU.mult, ALU.add), s["qm_sq"])
            eng.wait_ge(s["qm_r"], 1)
            for i, src in enumerate((qm, km)):
                f = src.rearrange("p t h d -> p (t h) d")
                do(tt(f, f, bc(rrm[:, 8 * i:8 * i + 8], 2, MD), ALU.mult), s["qm_n"])

            full(("hid",))
            hid = B(("hid",))[:, 0:64].rearrange("p (j c) -> p j c", j=2)
            do(tt(hbias, hid[:, :, 30], V("cmp_b1"), ALU.add))
            settle()
            free(tt(hx, hid[:, :, 0:30], bc(hbias, 2, 30), ALU.add), ("hid",))
            settle()
            do(tt(hu, hx, hx, ALU.mult))
            settle()
            do(ts(hu, hu, 0.044715, 1.0, ALU.mult, ALU.add))
            settle()
            do(tt(hu, hu, hx, ALU.mult), s["tanh_in"])
            eng.wait_ge(s["tanh_out"], 1)
            do(stt(ge, hu, 1.0, hx, ALU.add, ALU.mult))
            settle()
            do(ts(ge, ge, 0.5, None, ALU.mult), s["ge_done"])
            full(("cmp2",))
            free(cp(ctok.rearrange("p j g d -> p (j g d)"), B(("cmp2",), NC)[:, 0:4 * DH]), ("cmp2",))
            settle()
            do(tt(csq, ctok[:, 0], ctok[:, 0], ALU.mult))
            settle()
            do(row_sum(cs2, csq))
            settle()
            do(ts(cs2, cs2, 1.0 / DH, EPS, ALU.mult, ALU.add), s["kc_sq"])
            eng.wait_ge(s["kc_r"], 1)
            do(tt(ctok[:, 0], ctok[:, 0], bc(cr2, 2, DH), ALU.mult))
            settle()
            do(tt(ctok[:, 0], ctok[:, 0], bc(kn0, 1, NG), ALU.mult))
            settle()
            rope(None, ctok[:, 0], crot, csq, C("ccos", parts=NC), C("csin", parts=NC), NG)
            do(tt(ctok[:, 0], crot, csq, ALU.add), s["kc_rot"])

            for w, dst, gain in (("q", qmT, "mq_n"), ("k", kmT, "mk_n")):
                for t in range(TT):
                    full(("memT", w, t))
                    free(ts(dst[:, :, t * P:(t + 1) * P], B(("memT", w, t)).rearrange("p (h n) -> p h n", h=MH),
                            V(gain, 0), None, ALU.mult), ("memT", w, t))
            eng.wait_ge(s["gate_raw"], 1)
            do(ts(gates, gates, 0.5, 0.5, ALU.mult, ALU.add))

            def front(u):
                kind, h0, t, nh, nt = UNITS[u]
                nk = nt * P or NC
                b = B(("scores", u))[:, 0:nh * nk].rearrange("p (h k) -> p h k", h=nh)
                sc = sb_s[:, u % 2, 0:nh * nk].rearrange("p (h k) -> p h k", h=nh)
                full(("scores", u))
                if kind == "mem":
                    free(cp(sc, b), ("scores", u))
                else:
                    mask = C("cmpneg", 2)[:, t] if kind == "cmp" else C("causal")[:, (2 - nt) * P:2 * P]
                    free(tt(sc, b, bc(mask, 1, nh), ALU.add), ("scores", u))
                settle()
                do(row_max(mx[:, u % 2, 0:nh], sc))
                settle()
                scale = (MD if kind == "mem" else DH) ** -0.5
                do(ts(nmx[:, u % 2, 0:nh], mx[:, u % 2, 0:nh], -scale, None, ALU.mult), s["m_ready"])

            def factor(u):
                kind, h0, t, nh, nt = UNITS[u]
                total, f = sm[:, u % 2, 0:nh], fac[:, u % 2, 0:nh]
                eng.wait_ge(s["e_ready"], u + 1)
                if kind == "cmp":
                    e = sb_e[:, u % 2, 0:nh * NC].rearrange("p (h k) -> p h k", h=nh)
                    do(tt(e, e, bc(C("cmpok", 2)[:, t], 1, nh), ALU.mult), s["cmp_ok"])
                    settle()
                    do(row_sum(total, e))
                    settle()
                    do(ts(total, total, 1e-30, None, ALU.max))
                    settle()
                do(eng.reciprocal(f, total))
                settle()
                if kind != "mem":
                    h = 4 * h0 if kind == "cmp" else h0
                    g3 = gates[:, t, :].rearrange("p (h b) -> p h b", b=3)
                    do(tt(f, f, g3[:, h:h + nh, ("cmp", "slc", "win").index(kind)], ALU.mult))
                    settle()

            def gather(u):
                kind, h0, t, nh, nt = UNITS[u]
                dv = MD if kind == "mem" else DH
                h = 4 * h0 if kind == "cmp" else h0
                full(("values", u))
                b = B(("values", u))[:, 0:nh * dv].rearrange("p (h d) -> p h d", h=nh)
                f = bc(fac[:, u % 2, 0:nh], 2, dv)
                if kind == "mem":
                    free(tt(omem[:, t, h:h + nh, :], b, f, ALU.mult), ("values", u))
                elif kind == "cmp":
                    free(tt(osum[:, t, h:h + nh, :], b, f, ALU.mult), ("values", u))
                else:
                    part = otmp[:, u % 2, 0:nh * dv].rearrange("p (h d) -> p h d", h=nh)
                    free(tt(part, b, f, ALU.mult), ("values", u))
                    settle()
                    do(tt(osum[:, t, h:h + nh, :], osum[:, t, h:h + nh, :], part, ALU.add))

            front(0)
            front(1)
            for u in range(len(UNITS)):
                factor(u)
                if u + 2 < len(UNITS):
                    front(u + 2)
                gather(u)
                if u == 3:
                    eng.wait_ge(s["R_zero"], 1)
                if 3 <= u < 10:
                    shift_mix(2 * (u - 3))
            settle()
            do(ts(stat[:, 6:7], stat[:, 0:1], 1.0, None, ALU.mult), s["values_done"])

            r_, k_, v_ = pp[:, 0:4, :], pp[:, 4:8, :], pp[:, 8:12, :]
            taken(eng, ("omT", 1))
            eng.wait_ge(s["wa_done"], 2)
            do(ts(pp[:, 13, :], pp[:, 13, :], 0.5, 0.5, ALU.mult, ALU.add), s["xg_done"])
            do(eng.memset(dE[:, :, 0:1], 0.0))
            do(eng.memset(pat, 0.0))
            settle()
            pat3 = pat.rearrange("p (a b) -> p a b", a=16)
            do(eng.memset(pat3[:, :, 0:1], 1.0))
            do(tt(kkn, k_, bc(V("k_k"), 2, S), ALU.mult))
            eng.wait_ge(s["decay_done"], 1)
            settle()
            do(eng.tensor_tensor_scan(Dc.rearrange("p a b -> p (a b)"), dE.rearrange("p a b -> p (a b)"), pat, 0.0,
                                      ALU.mult, ALU.add))
            do(tt(tmp, kkn, kkn, ALU.mult), s["k_sq"])
            taken(eng, ("up", "a", 1))
            do(ts(aa, aa, 0.5, 0.5, ALU.mult, ALU.add))
            taken(eng, ("ksum", 1))
            do(ts(Di, Di, 1e-12, None, ALU.max))
            settle()
            do(eng.reciprocal(Di, Di))
            do(tt(tmp, aa, bc(V("k_a"), 2, S), ALU.mult))
            settle()
            do(tt(kkn, kkn, Di, ALU.mult))
            do(tt(tmp, tmp, bc(omka, 2, S), ALU.add))
            settle()
            do(tt(k_, k_, tmp, ALU.mult))
            do(tt(aa, aa, kkn, ALU.mult))
            dnow = Dc[:, :, 1:CH + 1]
            dprev = Dc[:, :, 0:CH]

            def chunks(ap):
                return ap.rearrange("p j (c n) -> p (j c) n", n=CH)

            do(eng.reciprocal(chunks(Di), dnow))
            settle()
            do(tt(tmp, r_, k_, ALU.mult))
            settle()
            do(tt(tmp, tmp, bc(V("r_k"), 2, S), ALU.mult), s["rk_done"])
            for hh in range(2):
                lanes = slice(DH * hh, DH * hh + DH)

                def ch(ap):
                    return ap.rearrange("p (j c) n -> p j c n", j=4)[lanes]

                for j in range(4):
                    o = {w: til[w][:, 2 * j + hh, :].rearrange("p (c n) -> p c n", n=CH) for w in "abkr"}

                    def at(ap):
                        return ap[lanes, j, :].rearrange("p (c n) -> p c n", n=CH)

                    do(stt(o["a"], at(kkn), -1.0, ch(dprev)[:, j], ALU.mult, ALU.mult), s["tilde_done"])
                    do(tt(o["b"], at(aa), at(Di), ALU.mult), s["tilde_done"])
                    do(tt(o["k"], at(k_), at(Di), ALU.mult), s["tilde_done"])
                    do(tt(o["r"], at(r_), ch(dnow)[:, j], ALU.mult), s["tilde_done"])
                do(cp(DC.rearrange("p (j two) c -> p two j c", two=2)[:, hh],
                      ch(Dc)[:, :, :, CH:CH + 1].rearrange("p j c n -> p j (c n)")))
            for q in range(2):
                full(("bonus", q))
                free(tt(bon[:, 2 * q:2 * q + 2, :], B(("bonus", q)).rearrange("p (j s) -> p j s", j=2),
                        v_[:, 2 * q:2 * q + 2, :], ALU.mult), ("bonus", q))

            settle()
            do(cp(Tm, bc(ident, 1, 16)))
            settle()

            def four(ap, b):
                return ap[:, 4 * b:4 * b + 4, :]

            def bank4(job):
                return B(job).rearrange("p (h n) -> p h n", h=4)

            for b in range(4):
                full(("A", b))
                do(tt(four(Am, b), bank4(("A", b)), bc(C("low"), 1, 4), ALU.mult))
                free(eng.copy_predicated(four(Tm, b), bc(C("lo1"), 1, 4).bitcast(U32), bank4(("A", b))), ("A", b))
            for w, dst, mask in (("Kk", Kk, "upp"), ("Rb", Rb, "uppi"), ("Rk", Rk, "uppi")):
                for b in range(4):
                    full((w, b))
                    free(tt(four(dst, b), bank4((w, b)), bc(C(mask), 1, 4), ALU.mult), (w, b))
            for n in LEVELS:
                for b in range(4):
                    full(("MX", n, b))
                    free(eng.copy_predicated(four(Mm, b), bc(C(f"up{n}"), 1, 4).bitcast(U32), bank4(("MX", n, b))),
                         ("MX", n, b))
            for b in range(4):
                t, hq = divmod(b, 2)
                full(("rhat", b))
                r3 = til["r"][:, 4 * hq:4 * hq + 4, t * P:(t + 1) * P]
                free(tt(r3, r3, B(("rhat", b), DH).rearrange("p (h n) -> p h n", h=4), ALU.add), ("rhat", b))
            taken(eng, ("Q", 0))
            do(tt(Ss[:, 0], Qs[:, 0], bc(DC[:, :, 0], 2, DH), ALU.mult), s["state_done"])
            for c in (1, 2):
                taken(eng, ("Q", c))
                full(("state", c))
                free(tt(stmp, B(("state", c), DH).rearrange("p (h n) -> p h n", h=NH), Qs[:, c], ALU.add),
                     ("state", c))
                settle()
                do(tt(stmp, stmp, Ss[:, c - 1], ALU.add))
                settle()
                do(tt(Ss[:, c], stmp, bc(DC[:, :, c], 2, DH), ALU.mult), s["state_done"])
            for q in range(2):
                full(("mean", q))
                yv = yb[:, 2 * q:2 * q + 2, :]
                free(stt(yv, B(("mean", q)).rearrange("p (j s) -> p j s", j=2), -1.0 / DH, yv, ALU.mult, ALU.add),
                     ("mean", q))
            settle()
            do(tt(yq, yb, yb, ALU.mult), s["y_sq"])
            taken(eng, ("var", 1))
            do(eng.reciprocal(yq, yq))
            settle()
            do(tt(yb, yb, yq, ALU.mult))
            settle()
            do(tt(yb, yb, bc(V("ln_w"), 2, S), ALU.mult))
            settle()
            do(tt(yb, yb, bc(V("ln_b"), 2, S), ALU.add))
            settle()
            do(tt(yb, yb, bon, ALU.add))
            settle()
            do(tt(obT, yb, gg, ALU.mult), s["ob_done"])
            settle()

            for n in BRANCHES:
                for ct in range(0, KD, 2):
                    job = ("branch", n, ct)
                    full(job)
                    taken(eng, ("merge", n * KD + ct))
                    b = B(job).rearrange("p (j s) -> p j s", j=2)
                    g2 = tg[:, n * KD + ct:n * KD + ct + 2, :]
                    if n == 0:
                        free(stt(mixT[:, ct:ct + 2, :], g2, 1.0, b, ALU.add, ALU.mult), job)
                    else:
                        prod = mprod[:, ct // 2 % 2, :].rearrange("p (j s) -> p j s", j=2)
                        free(stt(prod, g2, 1.0, b, ALU.add, ALU.mult), job)
                        settle()
                        do(tt(mixT[:, ct:ct + 2, :], mixT[:, ct:ct + 2, :], prod, ALU.add), s["mix_done"])
            eng.wait_ge(s["late_in"], 32)

            def add_x(t, q):
                full(("out", t, q))
                xv = x1[:, t, q * 512:(q + 1) * 512]
                free(stt(xv, B(("out", t, q)), 0.5, xv, ALU.mult, ALU.add), ("out", t, q))

            def mean_square(t):
                settle()
                st = stat[:, 4 + t:5 + t]
                do(eng.tensor_tensor_reduce(mprod.rearrange("p a b -> p (a b)"), x1[:, t, :], x1[:, t, :], 1.0, 0.0,
                                            ALU.mult, ALU.add, st))
                settle()
                do(ts(st, st, 1.0 / D, EPS, ALU.mult, ALU.add), s["x1_sq"])

            def normed(t):
                eng.wait_ge(s["x1_r"], t + 1)
                do(ts(xn2[:, t, :], x1[:, t, :], rstd[:, 4 + t:5 + t], None, ALU.mult), s["xn2_done"])

            def channel_half(t):
                full(("h2T", 0, t))
                free(cp(h2T[:, 0:4, t * P:(t + 1) * P], B(("h2T", 0, t)).rearrange("p (k n) -> p k n", k=4)),
                     ("h2T", 0, t))

            def largest(t):
                full(("logits", t))
                free(cp(lg[:, t, :], B(("logits", t))[:, 0:NE]), ("logits", t))
                settle()
                do(eng.max(top[:, t, :], lg[:, t, :]))
                settle()
                do(eng.max_index(idx[:, t, :], top[:, t, :], lg[:, t, :]))

            add_x(0, 0)
            add_x(0, 1)
            mean_square(0)
            normed(0)
            add_x(1, 0)
            channel_half(0)
            add_x(1, 1)
            mean_square(1)
            normed(1)
            largest(0)
            channel_half(1)
            largest(1)
            settle()
            do(cp(idf, idx))
            do(tt(et, top[:, :, 0:TOPK], bc(top[:, :, 0], 2, TOPK), ALU.subtract), s["lg_ss"])
            settle()
            experts = bc(bc(C("experts"), 1, TOPK), 1, TT)
            do(tt(chosen, experts, bc(idf[:, :, 0:TOPK], 3, NE), ALU.is_equal))
            settle()
            do(row_sum(sel, chosen.rearrange("p t k e -> p t e k")), s["sel_done"])
            eng.wait_ge(s["lg_exp"], 1)
            do(row_sum(es, et))
            settle()
            do(eng.reciprocal(er, es))
            settle()
            do(tt(et, et, bc(er, 2, TOPK), ALU.mult))
            settle()
            do(tt(chosen, chosen, bc(et, 3, NE), ALU.mult))
            settle()
            do(row_sum(gat, chosen.rearrange("p t k e -> p t e k")), s["gat_done"])
            full(("rank",))
            rank = B(("rank",))[:, 0:TT * NE].rearrange("p (t e) -> p t e", t=TT)
            do(stt(rk1, rank, 1.0, sel, ALU.add, ALU.mult))
            settle()
            do(ts(rankR[:, :, 0:NE], rk1, -1.0, None, ALU.add))
            settle()
            for k in range(2):
                for t in range(TT):
                    ins_ = ts(Pk[:, t, k, :], C("slots"), rankR[:, t, k:k + 1], None, ALU.is_equal)
                    do(ins_, s["P_ready"]) if (k, t) == (1, TT - 1) else do(ins_)
            free(row_max(cm[:, 0:1], B(("rank",))[:, TT * NE:(TT + 1) * NE]), ("rank",))
            settle()
            for r in range(1, ROUNDS):
                do(ts(cm[:, r:r + 1], cm[:, 0:1], float(CAP * r), None, ALU.is_gt))
            settle()
            do(row_sum(cm[:, 4:5], cm[:, 1:ROUNDS]))
            settle()
            do(ts(nrounds, cm[:, 4:5], 1.0, None, ALU.add))
            for r in range(ROUNDS):
                if r:
                    do(ts(rankR[:, :, r * NE:(r + 1) * NE], rk1, -1.0 - CAP * r, None, ALU.add))
                do(ts(gateR[:, :, r * NE:(r + 1) * NE], gat, 0.5, None, ALU.mult))
            do(eng.memset(rankR[:, :, ROUNDS * NE:], -1.0))
            do(eng.memset(gateR[:, :, ROUNDS * NE:], 0.0))
            settle()
            eng.sem_inc(s["o_free"], 1)
            eng.sem_inc(s["t_out"], 1)
            eng.sem_inc(s["h_out"], 2)
            do(cp(nz, C("half")[:, 0:2]), s["scratch_free"])
            settle()

            def take(number):
                eng.wait_ge(s["g_full"], number)
                eng.tensor_tensor(xg.rearrange("p (b k) n -> p b k n", b=2),
                                  psum[:, 4:6, :].rearrange("p b (k n) -> p b k n", k=4),
                                  bc(V("g_ffn").rearrange("p (b k) -> p b k", b=2), 3, 2 * CAP),
                                  ALU.mult).then_inc(s["xg_ready"], 1)

            take(1)
            rounds = load_rounds(eng)
            with eng.Fori(0, rounds) as r:
                with eng.Fori(0, NE // 2) as i:
                    it = r * (NE // 2) + i
                    for k in range(2):
                        E = it * 2 + k
                        for t in range(TT):
                            for twice in range(2):
                                x_ = eng.tensor_scalar(PG[:, t, twice, :], C("slots"), rankR[:, t, bass.ds(E, 1)],
                                                       gateR[:, t, bass.ds(E, 1)], ALU.is_equal, ALU.mult)
                        x_.then_inc(s["pg_ready"], 1)
                        if k == 0:
                            for n in range(2):
                                for t in range(TT):
                                    x_ = eng.tensor_scalar(Pk[:, t, n, :], C("slots"),
                                                           rankR[:, t, bass.ds(it * 2 + (2 + n), 1)], None,
                                                           ALU.is_equal)
                            x_.then_inc(s["P_ready"], 1)
                        eng.wait_ge(s["t_full"], E * 5 + 1)
                        eng.tensor_copy(pgt[:, k, :], psum[:, 5, 0:S]).then_inc(s["t_out"], 1)
                        for q in range(4):
                            hf = q % 2
                            eng.wait_ge(s["t_full"], E * 5 + (q + 2))
                            bias = b1_sb[:, bass.ds(i * 2 + k, 1), 4 * q:4 * q + 4].rearrange("p e n -> p (e n)")
                            eng.tensor_tensor(hb[:, hf, :].rearrange("p (a n) -> p a n", a=4),
                                              psum[:, 5, 0:4 * CAP].rearrange("p (a n) -> p a n", a=4),
                                              bc(bias, 2, CAP), ALU.add).then_inc(s["t_out"], 1)
                            eng.wait_ge(s["t_out"], E * 5 + (q + 3))
                            eng.tensor_scalar(xlo[:, hf, :], hb[:, hf, 0:2 * CAP], 7.0, None, ALU.min
                                              ).then_inc(s["x_ready"], 1)
                            eng.tensor_scalar(xhi[:, hf, :], hb[:, hf, 2 * CAP:4 * CAP], 7.0, -7.0, ALU.min, ALU.max
                                              ).then_inc(s["v2_step"], 1)
                            eng.wait_ge(s["t_ready"], E * 4 + (q + 1))
                            eng.scalar_tensor_tensor(out=th[:, hf, :], in0=th[:, hf, :], scalar=1.0,
                                                     in1=xlo[:, hf, :], op0=ALU.add, op1=ALU.mult
                                                     ).then_inc(s["v2_step"], 1)
                            eng.wait_ge(s["v2_step"], E * 8 + (2 * q + 2))
                            eng.scalar_tensor_tensor(
                                out=act[:, 2 * q:2 * q + 2, :].rearrange("p a n -> p (a n)"), in0=xhi[:, hf, :],
                                scalar=1.0, in1=th[:, hf, :], op0=ALU.add, op1=ALU.mult).then_inc(s["a_ready"], 1)
                        if k == 1:
                            take(it + 2)
            for t in range(TT):
                eng.wait_ge(s["y_full"], t + 1)
                eng.tensor_tensor(x1[:, t, :].rearrange("p (a n) -> p a n", a=2), psum[:, 2 * t:2 * t + 2, :],
                                  x1[:, t, :].rearrange("p (a n) -> p a n", a=2), ALU.add).then_inc(s["y_out"], 1)

        @block.scalar
        def _(eng):
            a = Steps(eng, s["a_step"], bank_free, bank_full)
            do, free, full, settle = a.do, a.free, a.full, a.settle
            act_, cp = eng.activation, eng.copy

            def halves(job, n=2):
                return B(job).rearrange("p (j s) -> p j s", j=n)

            def shift(ct):
                full(("shift", ct))
                free(cp(pbuf[:, ct:ct + 2, 1:S + 1], halves(("shift", ct))), ("shift", ct))

            def merge(ct):
                full(("merge", ct))
                for c in range(2):
                    ins_ = act_(tg[:, ct + c, :], halves(("merge", ct))[:, c, :], ACT.Tanh,
                                bias=hbm[:, ct + c:ct + c + 1], scale=0.5)
                    free(ins_, ("merge", ct)) if c else do(ins_)

            for t in range(TT):
                full(("q", t))
                free(cp(qk[:, t, 0:NH, :].rearrange("p h d -> p (h d)"), B(("q", t))), ("q", t))
            for t in range(TT):
                full(("kc", t))
                do(cp(qk[:, t, NH:12, :].rearrange("p h d -> p (h d)"), B(("kc", t))[:, 0:256]))
                free(cp(kcv[:, t].rearrange("p j n -> p (j n)"), B(("kc", t))[:, 256:512]), ("kc", t))
            for t in range(TT):
                full(("vg", t))
                free(cp(vg[:, t, :], B(("vg", t))[:, 0:280]), ("vg", t))
            for w, dst in (("qm", qm), ("km", km), ("vm", vm)):
                for t in range(TT):
                    full((w, t))
                    free(cp(dst[:, t].rearrange("p h d -> p (h d)"), B((w, t))), (w, t))
            settle()
            do(act_(gates, vg[:, :, 256:280], ACT.Tanh, scale=0.5), s["gate_raw"])
            shift(0)
            eng.wait_ge(s["tanh_in"], 1)
            do(act_(hu, hu, ACT.Tanh, scale=0.7978845608028654), s["tanh_out"])
            shift(2)
            shift(4)
            full(("cT",))
            free(cp(kcT, B(("cT",), DH)[:, 0:2 * NC].rearrange("p (g c) -> p g c", g=2)), ("cT",))
            for t in range(TT):
                for q in range(3):
                    full(("qkT", t, q))
                    free(cp(qkT[:, 4 * q:4 * q + 4, t * P:(t + 1) * P],
                            B(("qkT", t, q), DH).rearrange("p (h n) -> p h n", h=4)), ("qkT", t, q))

            def filler(u):
                kind, ct = FILL[FILL_UNITS.index(u) // 2]
                (shift if kind == "shift" else merge)(ct)

            def exps(u):
                kind, h0, t, nh, nt = UNITS[u]
                nk = nt * P or NC
                scale = (MD if kind == "mem" else DH) ** -0.5
                eng.wait_ge(s["m_ready"], u + 1)
                for h in range(nh):
                    ins_ = act_(sb_e[:, u % 2, h * nk:(h + 1) * nk], sb_s[:, u % 2, h * nk:(h + 1) * nk], ACT.Exp,
                                bias=nmx[:, u % 2, h:h + 1], scale=scale, accum_out=sm[:, u % 2, h:h + 1])
                    do(ins_, s["e_ready"]) if h == nh - 1 else do(ins_)

            exps(0)
            exps(1)
            for u in range(len(UNITS)):
                full(("turn", u))
                if u >= 2:
                    full(("values", u - 2))
                rows = P if UNITS[u][4] else NC
                free(cp(sb_eT[0:rows, u % 2, :], B(("turn", u), rows)), ("turn", u))
                if u + 2 < len(UNITS):
                    exps(u + 2)
                if u - 1 in FILL_UNITS[1::2]:
                    filler(u - 1)
            if FILL_UNITS[-1] == len(UNITS) - 1:
                filler(FILL_UNITS[-1])
            for w, dst in (("oaT", oaT), ("omT", omT)):
                for t in range(TT):
                    full((w, t))
                    free(cp(dst[:, :, t * P:(t + 1) * P], B((w, t)).rearrange("p (c n) -> p c n", c=4)), (w, t))

            eng.wait_ge(s["tables_in"], 16)
            eng.wait_ge(s["pp_done"], 14)
            do(act_(pp[0:DH, 12, :], pp[0:DH, 12, :], ACT.Tanh), s["wa_done"])
            do(act_(pp[:, 13, :], pp[:, 13, :], ACT.Tanh, scale=0.5), s["wa_done"])
            for q in range(2):
                full(("up", "w", q))
                for c in range(2):
                    ins_ = act_(tmp[:, 2 * q + c, :], halves(("up", "w", q))[:, c, :], ACT.Tanh,
                                bias=hw0[:, 2 * q + c:2 * q + c + 1], scale=0.5)
                    free(ins_, ("up", "w", q)) if c else do(ins_)
            settle()
            do(act_(tmp, tmp, ACT.Copy, scale=-EM05 / 2, bias=-EM05 / 2))
            settle()
            do(act_(dE[:, :, 1:CH + 1], tmp.rearrange("p j (c n) -> p (j c) n", n=CH), ACT.Exp), s["decay_done"])
            for q in range(2):
                full(("up", "a", q))
                for c in range(2):
                    ins_ = act_(aa[:, 2 * q + c, :], halves(("up", "a", q))[:, c, :], ACT.Tanh,
                                bias=ha0[:, 2 * q + c:2 * q + c + 1], scale=0.5)
                    free(ins_, ("up", "a", q)) if c else do(ins_)
            for q in range(2):
                full(("up", "g", q))
                free(cp(gg[:, 2 * q:2 * q + 2, :], halves(("up", "g", q))), ("up", "g", q))
            for q in range(2):
                full(("ksum", q))
                free(act_(Di[:, 2 * q:2 * q + 2, :], halves(("ksum", q)), ACT.Sqrt), ("ksum", q))
            for ct in MERGES["ksum"]:
                merge(ct)
            for t in range(TT):
                full(("vtok", t))
                free(cp(tok["v"][:, t].rearrange("p h d -> p (h d)"), B(("vtok", t))), ("vtok", t))
            for w in "akb":
                for t in range(TT):
                    full(("tok", w, t))
                    b = B(("tok", w, t)).rearrange("p (h d) -> p h d", h=NH)
                    dst = KA[:, t * NH:(t + 1) * NH, DH:P] if w == "a" else tok[w][:, t]
                    free(cp(dst, b), ("tok", w, t))
            for b in range(4):
                full(("M1", b))
                free(cp(Mm[:, 4 * b:4 * b + 4, :], B(("M1", b)).rearrange("p (h n) -> p h n", h=4)), ("M1", b))
            for t in range(TT):
                full(("KV", t))
                free(cp(KA[:, t * NH:(t + 1) * NH, 0:DH], B(("KV", t)).rearrange("p (h d) -> p h d", h=NH)), ("KV", t))
            for n in LEVELS:
                for b in range(4):
                    full(("X", n, b))
                    free(cp(Xm[:, b, :], B(("X", n, b))), ("X", n, b))
                for b in range(4) if n > 2 else ():
                    full(("TT", n, b))
                    free(cp(Tm[:, 4 * b:4 * b + 4, :], B(("TT", n, b)).rearrange("p (h n) -> p h n", h=4)),
                         ("TT", n, b))
            for b in range(4):
                full(("UW", b))
                free(cp(UW[:, 4 * b:4 * b + 4, :], B(("UW", b)).rearrange("p (h n) -> p h n", h=4)), ("UW", b))
            for w, c in (("Q", 0), ("Q", 1), ("PT", 1), ("Q", 2), ("PT", 2)):
                full((w, c))
                dst = Qs if w == "Q" else PT
                free(cp(dst[:, c], B((w, c), DH).rearrange("p (h n) -> p h n", h=NH)), (w, c))
            for ct in MERGES["state"]:
                merge(ct)
            for t in range(TT):
                full(("Y", t))
                free(cp(yb[:, :, t * P:(t + 1) * P], B(("Y", t)).rearrange("p (j n) -> p j n", j=4)), ("Y", t))
            for ct in MERGES["Y"]:
                merge(ct)
            for q in range(2):
                full(("var", q))
                free(act_(yq[:, 2 * q:2 * q + 2, :], halves(("var", q)), ACT.Sqrt, scale=1.0 / DH,
                          bias=C("gn_eps")), ("var", q))

            for t in range(TT):
                full(("h2T", 1, t))
                free(cp(h2T[:, 4:8, t * P:(t + 1) * P], B(("h2T", 1, t)).rearrange("p (k n) -> p k n", k=4)),
                     ("h2T", 1, t))
            eng.wait_ge(s["lg_ss"], 1)
            do(act_(et, et, ACT.Exp), s["lg_exp"])
            full(("gateT",))
            free(cp(gT[0:NE, :], B(("gateT",), NE)[:, 0:S]), ("gateT",))

            rounds = load_rounds(eng)
            with eng.Fori(0, rounds) as r:
                with eng.Fori(0, NE // 2) as i:
                    for k in range(2):
                        E = (r * (NE // 2) + i) * 2 + k

                        def evacuate(q):
                            eng.wait_ge(s["h_full"], E * 4 + (q + 1))
                            cp(hraw[:, q % 2, :], psum[:, 6 + q % 2, :]).then_inc(s["h_out"], 1)

                        evacuate(0)
                        for q in range(4):
                            if q < 3:
                                evacuate(q + 1)
                            eng.wait_ge(s["x_ready"], E * 4 + (q + 1))
                            act_(th[:, q % 2, :], xlo[:, q % 2, :], ACT.Tanh, scale=1.702 / 2
                                 ).then_inc(s["t_ready"], 1)
                        eng.wait_ge(s["o_full"], E + 1)
                        cp(osb, psum[:, 4:6, :].rearrange("p a n -> p (a n)")).then_inc(s["o_free"], 1)

        @block.tensor
        def _(pe):
            def use(job):
                b, used = BANK[job]
                if used:
                    pe.wait_ge(bank_free[b], used)

            def fill(ins_, job):
                ins_.then_inc(bank_full[BANK[job][0]], 1)

            def weights(name):
                n = W1_AT[name]
                pe.wait_ge(unit_in[n % N1], 16 * (n // N1 + 1))
                return slots[n % N1]

            def mm(o, lhsT, rhs, start=True, stop=True):
                return pe.matmul(o, lhsT, rhs, start=start, stop=stop, skip_group_check=True)

            def turn(o, in_):
                return pe.transpose(o, in_, ident[0:in_.shape[0], 0:in_.shape[0]])

            def rows_turned(w, src, number):
                for t in range(TT):
                    pe.wait_ge(s["xn_done"], 2 * number + t + 1)
                    for q in range(2):
                        job = (w, q, t)
                        use(job)
                        for k in range(4):
                            last = turn(B(job)[:, k * P:(k + 1) * P],
                                        src[:, t, (4 * q + k) * P:(4 * q + k + 1) * P])
                        fill(last, job)

            def channels(job, unit, c0, c):
                w = weights(unit).rearrange("p (k n) -> p k n", k=KD)
                if c == 0:
                    use(job)
                for k in range(KD):
                    last = mm(B(job)[:, c * S:(c + 1) * S], w[:, k, (c0 + c) * P:(c0 + c + 1) * P], hT[:, k, :],
                              k == 0, k == KD - 1)
                if c == 1:
                    fill(last, job)

            def shift(ct):
                for c in range(2):
                    channels(("shift", ct), f"shift{ct // 4}", ct % 4, c)

            def merge(ct, c):
                channels(("merge", ct), f"merge{ct // 4}", ct % 4, c)

            def merges(where):
                for ct in MERGES[where]:
                    for c in range(2):
                        merge(ct, c)

            def token_rows(name):
                w = weights(name).rearrange("p (k n) -> p k n", k=KD)
                src = mT if name in ("km", "vm") else hT
                width = 280 if name == "vg" else 512
                for t in range(TT):
                    use((name, t))
                    for k in range(KD):
                        last = mm(B((name, t))[:, 0:width], src[:, k, t * P:(t + 1) * P], w[:, k, 0:width],
                                  k == 0, k == KD - 1)
                    fill(last, (name, t))

            pe.wait_ge(s["const_in"], 32)
            rows_turned("hT", xs, 0)
            for t in range(TT):
                for q in range(2):
                    taken(pe, ("hT", q, t))
            token_rows("q")
            rows_turned("mT", ms, 1)
            for name in ("kc", "vg", "qm"):
                token_rows(name)
            use(("kcT",))
            taken(pe, ("kc", 1))
            for j in range(2):
                for t in range(TT):
                    last = turn(B(("kcT",))[:, j * S + t * P:j * S + (t + 1) * P], kcv[:, t, j, :])
            fill(last, ("kcT",))
            for t in range(TT):
                for q in range(2):
                    taken(pe, ("mT", q, t))
            token_rows("km")
            token_rows("vm")
            use(("hid",))
            taken(pe, ("kcT",))
            pe.wait_ge(s["small_in"], 144)
            w = weights("cmp1").rearrange("p (j l n) -> p j l n", j=2, l=16)
            for j in range(2):
                for l in range(16):
                    last = mm(B(("hid",))[:, j * 32:j * 32 + 31], w[:, j, l, :], R[:, j, l, :], l == 0, l == 15)
            fill(last, ("hid",))
            shift(0)
            shift(2)
            use(("cmp2",))
            pe.wait_ge(s["ge_done"], 1)
            for j in range(2):
                for g in range(NG):
                    last = mm(B(("cmp2",), NC)[:, (2 * j + g) * DH:(2 * j + g + 1) * DH],
                              ge[:, j, g * NC:(g + 1) * NC], cw2[:, j, :])
            fill(last, ("cmp2",))
            shift(4)
            use(("cT",))
            pe.wait_ge(s["kc_rot"], 1)
            for g in range(NG):
                last = turn(B(("cT",), DH)[:, g * NC:(g + 1) * NC], ctok[:, 0, g, :])
            fill(last, ("cT",))
            for t in range(TT):
                pe.wait_ge(s["qk_rot"], t + 1)
                for q in range(3):
                    use(("qkT", t, q))
                    for h in range(4):
                        last = turn(B(("qkT", t, q), DH)[:, h * P:(h + 1) * P], qk[:, t, 4 * q + h, :])
                    fill(last, ("qkT", t, q))
            pe.wait_ge(s["qm_n"], 2)
            for w, src in (("q", qm), ("k", km)):
                for t in range(TT):
                    use(("memT", w, t))
                    for h in range(MH):
                        last = turn(B(("memT", w, t))[:, h * P:(h + 1) * P], src[:, t, h, :])
                    fill(last, ("memT", w, t))
            taken(pe, ("cT",))
            for t in range(TT):
                for q in range(3):
                    taken(pe, ("qkT", t, q))

            def scores(u):
                kind, h0, t, nh, nt = UNITS[u]
                nk = nt * P or NC
                use(("scores", u))
                if kind == "mem" and UNITS[u - 1][0] != "mem":
                    for w in "qk":
                        for part in range(TT):
                            taken(pe, ("memT", w, part))
                for h in range(nh):
                    if kind == "mem":
                        q_, k_ = qmT[:, h0 + h, t * P:(t + 1) * P], kmT[:, h0 + h, 0:nk]
                    elif kind == "cmp":
                        q_, k_ = qkT[:, 4 * h0 + h, t * P:(t + 1) * P], kcT[:, h0, :]
                    else:
                        kv = NH + (0 if kind == "slc" else NG) + h0 // 4
                        q_, k_ = qkT[:, h0 + h, t * P:(t + 1) * P], qkT[:, kv, 0:nk]
                    last = mm(B(("scores", u))[:, h * nk:(h + 1) * nk], q_, k_)
                fill(last, ("scores", u))

            scores(0)
            scores(1)
            for u, (kind, h0, t, nh, nt) in enumerate(UNITS):
                use(("turn", u))
                pe.wait_ge(s["e_ready"], u + 1)
                if kind == "cmp":
                    pe.wait_ge(s["cmp_ok"], u + 1)
                rows = P if nt else NC
                for b in range(4):
                    last = turn(B(("turn", u), rows)[:, b * P:(b + 1) * P], sb_e[:, u % 2, b * rows:(b + 1) * rows])
                fill(last, ("turn", u))
                if u + 2 < len(UNITS):
                    scores(u + 2)
                use(("values", u))
                taken(pe, ("turn", u))
                dv = MD if kind == "mem" else DH
                for h in range(nh):
                    for kt in range(nt or 1):
                        if kind == "mem":
                            val = vm[:, kt, h0 + h, :]
                        elif kind == "cmp":
                            val = ctok[:, 1, h0, :]
                        else:
                            c = (0 if kind == "slc" else P) + h0 // 4 * DH
                            val = vg[:, kt, c:c + DH]
                        blk = h * (nt or 1) + kt
                        last = mm(B(("values", u))[:, h * dv:(h + 1) * dv],
                                  sb_eT[0:rows, u % 2, blk * P:(blk + 1) * P], val, kt == 0, kt == (nt or 1) - 1)
                fill(last, ("values", u))
                if u in FILL_UNITS:
                    number = FILL_UNITS.index(u)
                    name, ct = FILL[number // 2]
                    channels((name, ct), f"{name}{ct // 4}", ct % 4, number % 2)
            pe.wait_ge(s["values_done"], 1)
            for w, src in (("oaT", osum), ("omT", omem)):
                for t in range(TT):
                    use((w, t))
                    flat = src[:, t].rearrange("p h d -> p (h d)")
                    for c in range(4):
                        last = turn(B((w, t))[:, c * P:(c + 1) * P], flat[:, c * P:(c + 1) * P])
                    fill(last, (w, t))

            pe.wait_ge(s["tables_in"], 16)
            for w in "wag":
                if w == "w":
                    pe.wait_ge(s["wa_done"], 1)
                if w == "g":
                    pe.wait_ge(s["xg_done"], 1)
                lanes = {"w": slice(0, DH), "a": slice(DH, P), "g": slice(0, P)}[w]
                for q in range(2):
                    use(("up", w, q))
                    for c in range(2):
                        ct = 2 * q + c
                        last = mm(B(("up", w, q))[:, c * S:(c + 1) * S],
                                  (up_g if w == "g" else up_w)[lanes, ct * P:(ct + 1) * P],
                                  pp[lanes, 13 if w == "g" else 12, :])
                    fill(last, ("up", w, q))
            flat = tmp.rearrange("p j s -> p (j s)")
            for w, ready in (("ksum", s["k_sq"]), ("bonus", s["rk_done"])):
                pe.wait_ge(ready, 1)
                for q in range(2):
                    use((w, q))
                    fill(mm(B((w, q)), C("heads"), flat[:, q * 512:(q + 1) * 512]), (w, q))
                if w == "ksum":
                    merges("ksum")
            for t in range(TT):
                use(("vtok", t))
                for j in range(4):
                    last = turn(B(("vtok", t))[:, j * P:(j + 1) * P], pp[:, 8 + j, t * P:(t + 1) * P])
                fill(last, ("vtok", t))
            pe.wait_ge(s["tilde_done"], 32)
            for w in "akb":
                for t in range(TT):
                    use(("tok", w, t))
                    for h in range(NH):
                        last = turn(B(("tok", w, t))[:, h * DH:(h + 1) * DH], til[w][:, h, t * P:(t + 1) * P])
                    fill(last, ("tok", w, t))
            for w, left, right in (("A", "a", "b"), ("Kk", "k", "a"), ("Rb", "b", "r"),
                                   ("Rk", "k", "r")):
                for b in range(4):
                    t, hq = divmod(b, 2)
                    use((w, b))
                    for h in range(4):
                        tok_ = slice(t * P, (t + 1) * P)
                        last = mm(B((w, b))[:, h * P:(h + 1) * P], til[left][:, 4 * hq + h, tok_],
                                  til[right][:, 4 * hq + h, tok_])
                    fill(last, (w, b))
            for b in range(4):
                use(("M1", b))
                taken(pe, ("A", b))
                for h in range(4):
                    last = turn(B(("M1", b))[:, h * P:(h + 1) * P], Tm[:, 4 * b + h, :])
                fill(last, ("M1", b))
            for t in range(TT):
                use(("KV", t))
                for b in range(2):
                    taken(pe, ("Kk", 2 * t + b))
                taken(pe, ("vtok", t))
                for h in range(NH):
                    last = mm(B(("KV", t))[:, h * DH:(h + 1) * DH], Kk[:, t * NH + h, :], tok["v"][:, t, h, :])
                fill(last, ("KV", t))

            for n in LEVELS:
                for b in range(4):
                    use(("X", n, b))
                    taken(pe, ("MX", n // 2, b) if n > 2 else ("M1", b))
                    for h in range(4):
                        last = mm(B(("X", n, b))[:, h * P:(h + 1) * P], Am[:, 4 * b + h, :], Mm[:, 4 * b + h, :])
                    fill(last, ("X", n, b))
                for b in range(4) if n > 2 else ():
                    use(("TT", n, b))
                    for h in range(4):
                        last = turn(B(("TT", n, b))[:, h * P:(h + 1) * P], Mm[:, 4 * b + h, :])
                    fill(last, ("TT", n, b))
                for b in range(4):
                    use(("MX", n, b))
                    taken(pe, ("X", n, b))
                    if n > 2:
                        taken(pe, ("TT", n, b))
                    for h in range(4):
                        last = mm(B(("MX", n, b))[:, h * P:(h + 1) * P], Tm[:, 4 * b + h, :],
                                  Xm[:, b, h * P:(h + 1) * P])
                    fill(last, ("MX", n, b))
            for b in range(4):
                use(("UW", b))
                taken(pe, ("MX", 32, b))
                taken(pe, ("KV", b // 2))
                for h in range(4):
                    last = mm(B(("UW", b))[:, h * P:(h + 1) * P], Mm[:, 4 * b + h, :], KA[:, 4 * b + h, :])
                fill(last, ("UW", b))
            for b in range(4):
                use(("rhat", b))
                taken(pe, ("UW", b))
                for h in range(4):
                    last = mm(B(("rhat", b), DH)[:, h * P:(h + 1) * P], UW[:, 4 * b + h, DH:P], Rb[:, 4 * b + h, :])
                fill(last, ("rhat", b))
            for w, c in (("Q", 0), ("Q", 1), ("PT", 1), ("Q", 2), ("PT", 2)):
                t, lanes = c // 2, slice(DH * (c % 2), DH * (c % 2) + DH)
                use((w, c))
                for h in range(NH):
                    o = B((w, c), DH)[:, h * DH:(h + 1) * DH]
                    uw, b_, k_, v_ = (UW[lanes, t * NH + h, :], tok["b"][lanes, t, h, :], tok["k"][lanes, t, h, :],
                                      tok["v"][lanes, t, h, :])
                    if w == "Q":
                        mm(o, b_, uw[:, 0:DH], True, False)
                        last = mm(o, k_, v_, False, True)
                    else:
                        last = mm(o, uw[:, DH:P], b_)
                fill(last, (w, c))
            for c in (1, 2):
                merge(MERGES["state"][0], c - 1)
                use(("state", c))
                taken(pe, ("PT", c))
                pe.wait_ge(s["state_done"], c)
                for h in range(NH):
                    last = mm(B(("state", c), DH)[:, h * DH:(h + 1) * DH], PT[:, c, h, :], Ss[:, c - 1, h, :])
                fill(last, ("state", c))
            for b in range(4):
                taken(pe, ("rhat", b))
            for t in range(TT):
                pe.wait_ge(s["state_done"], 2 * t + 1)
                use(("Y", t))
                for h in range(NH):
                    j, hh = divmod(h, 2)
                    lanes = slice(DH * hh, DH * hh + DH)
                    o = psum[lanes, BANK[("Y", t)][0], j * P:(j + 1) * P]
                    mm(o, tok["v"][:, t, h, :], Rk[:, t * NH + h, :], True, False)
                    mm(o, UW[:, t * NH + h, 0:DH], Rb[:, t * NH + h, :], False, False)
                    for half in range(2):
                        c = 2 * t + half
                        if c:
                            last = mm(o[:, half * CH:(half + 1) * CH], Ss[:, c - 1, h, :],
                                      til["r"][:, h, c * CH:(c + 1) * CH], False, True)
                fill(last, ("Y", t))
            merge(MERGES["Y"][0], 0)
            for t in range(TT):
                taken(pe, ("Y", t))
            for w, src in (("mean", yb), ("var", yq)):
                if w == "var":
                    merge(MERGES["Y"][0], 1)
                    pe.wait_ge(s["y_sq"], 1)
                flat = src.rearrange("p j s -> p (j s)")
                for q in range(2):
                    use((w, q))
                    fill(mm(B((w, q)), C("heads"), flat[:, q * 512:(q + 1) * 512]), (w, q))

            taken(pe, ("oaT", 1))
            taken(pe, ("omT", 1))
            for n in BRANCHES:
                src = (oaT, obT, omT)[n]
                if n == 1:
                    pe.wait_ge(s["ob_done"], 1)
                w = weights(f"branch{n}").rearrange("p (c n) -> p c n", c=4)
                for ct in range(0, KD, 2):
                    job = ("branch", n, ct)
                    use(job)
                    for c in range(2):
                        for k in range(4):
                            last = mm(B(job)[:, c * S:(c + 1) * S], w[:, k, (ct + c) * P:(ct + c + 1) * P],
                                      src[:, k, :], k == 0, k == 3)
                    fill(last, job)
            pe.wait_ge(s["out_in"], 32)
            w = [out_w[n].rearrange("p (c n) -> p c n", c=4) for n in range(2)]

            def out_rows(t, q):
                job = ("out", t, q)
                use(job)
                for k in range(KD):
                    if (t, q) == (0, 0) and k % 2 == 0:
                        pe.wait_ge(s["mix_done"], KD // 2 + k // 2 + 1)
                    last = mm(B(job), mixT[:, k, t * P:(t + 1) * P], w[k // 4][:, k % 4, q * 512:(q + 1) * 512],
                              k == 0, k == KD - 1)
                fill(last, job)

            def xn2_turned(t):
                pe.wait_ge(s["xn2_done"], t + 1)
                for q in range(2):
                    job = ("h2T", q, t)
                    use(job)
                    for k in range(4):
                        last = turn(B(job)[:, k * P:(k + 1) * P], xn2[:, t, (4 * q + k) * P:(4 * q + k + 1) * P])
                    fill(last, job)

            def logits(t):
                use(("logits", t))
                for q in range(2):
                    taken(pe, ("h2T", q, t))
                o = B(("logits", t))[:, 0:NE]
                for k in range(KD):
                    mm(o, h2T[:, k, t * P:(t + 1) * P], router_w[:, k, :], k == 0, False)
                fill(mm(o, C("ones")[0:1, :], router_b[0:1, :], False, True), ("logits", t))

            out_rows(0, 0)
            out_rows(0, 1)
            out_rows(1, 0)
            xn2_turned(0)
            out_rows(1, 1)
            pe.wait_ge(s["router_ready"], 1)
            logits(0)
            xn2_turned(1)
            logits(1)
            use(("rank",))
            pe.wait_ge(s["sel_done"], 1)
            o = B(("rank",))
            mm(o[:, 0:NE], C("before"), sel[:, 0, :])
            mm(o[:, NE:2 * NE], C("ones"), sel[:, 0, :], True, False)
            mm(o[:, NE:2 * NE], C("before"), sel[:, 1, :], False, True)
            mm(o[:, 2 * NE:3 * NE], C("ones"), sel[:, 0, :], True, False)
            fill(mm(o[:, 2 * NE:3 * NE], C("ones"), sel[:, 1, :], False, True), ("rank",))
            use(("gateT",))
            pe.wait_ge(s["gat_done"], 1)
            for t in range(TT):
                last = turn(B(("gateT",), NE)[:, t * P:(t + 1) * P], gat[:, t, :])
            fill(last, ("gateT",))

            def gather(half):
                for d in range(4 * half, 4 * half + 4):
                    for t in range(TT):
                        last = mm(psum[:, 4 + d // 4, d % 4 * P:(d % 4 + 1) * P], xn2[:, t, d * P:(d + 1) * P],
                                  Pk[:, t].rearrange("p k n -> p (k n)"), t == 0, t == TT - 1)
                if half:
                    last.then_inc(s["g_full"], 1)

            def scatter(k, done=None):
                for t in range(TT):
                    for h in range(2):
                        last = mm(psum[:, 2 * t + h, :], pgt[:, k, t * P:(t + 1) * P],
                                  osb[:, h * 512:(h + 1) * 512], False, False)
                    if done is not None:
                        last.then_inc(done, 1)

            pe.wait_ge(s["P_ready"], 1)
            for b in range(4, 6):
                pe.wait_ge(bank_free[b], LAST_USE[b])
            gather(0)
            gather(1)
            for b in range(NB):
                pe.wait_ge(bank_free[b], LAST_USE[b])
            for t in range(TT):
                for h in range(2):
                    mm(psum[:, 2 * t + h, :], gT[0:NE, t * P:(t + 1) * P], b2_sb[0:NE, h * 512:(h + 1) * 512],
                       True, False)
            pe.wait_ge(s["zeros_done"], 2)
            rounds = load_rounds(pe)
            with pe.Fori(0, rounds) as r:
                with pe.Fori(0, NE // 2) as i:
                    it = r * (NE // 2) + i
                    for k in range(2):
                        E = it * 2 + k

                        def up(q):
                            pe.wait_ge(expert_in[q][k], (it if q in TWICE else E) * 16 + 16)
                            pe.wait_ge(s["h_out"], E * 4 + (q + 1))
                            w = w1_slots[q][k].rearrange("p (k n) -> p k n", k=KD)
                            for d in range(KD):
                                half = d % 2
                                last = mm(psum[CAP * half:CAP * half + CAP, 6 + q % 2, :],
                                          xg[:, d, CAP * k:CAP * k + CAP], w[:, d, :], d < 2, d >= KD - 2)
                            last.then_inc(s["h_full"], 1)

                        def turn_up(q):
                            pe.wait_ge(s["h_out"], E * 4 + (q + 3))
                            pe.wait_ge(s["t_out"], E * 5 + (q + 2))
                            for c in range(4):
                                last = mm(psum[:, 5, c * CAP:(c + 1) * CAP], hraw[:, q % 2, c * P:(c + 1) * P],
                                          C("twice"))
                            last.then_inc(s["t_full"], 1)

                        if k == 0:
                            pe.wait_ge(s["xg_ready"], it + 1)
                        up(0)
                        pe.wait_ge(s["o_free"], E + 1)
                        pe.wait_ge(s["pg_ready"], E + 1)
                        pe.wait_ge(s["t_out"], E * 5 + 1)
                        for t in range(TT):
                            last = turn(psum[:, 5, t * P:(t + 1) * P], PG[:, t].rearrange("p k n -> p (k n)"))
                        last.then_inc(s["t_full"], 1)
                        up(1)
                        turn_up(0)
                        up(2)
                        turn_up(1)
                        up(3)
                        turn_up(2)
                        if k == 1:
                            pe.wait_ge(s["P_ready"], it + 2)
                            gather(0)
                        turn_up(3)
                        pe.wait_ge(s["t_out"], E * 5 + 6)
                        if k == 1:
                            gather(1)
                        scatter(1 - k)
                        pe.wait_ge(s["a_ready"], E * 4 + 4)
                        if k == 1:
                            pe.wait_ge(s["xg_ready"], it + 2)
                        for part in range(2):
                            pe.wait_ge(expert_in[W2_AT + part][k], it * 16 + 16)
                            w = w2_slots[part][k].rearrange("p (c n) -> p c n", c=4)
                            for h in range(2):
                                for c in range(4):
                                    half = c % 2
                                    last = mm(psum[CAP * half:CAP * half + CAP, 4 + h, :], act[:, 4 * part + c, :],
                                              w[:, c, h * 512:(h + 1) * 512], part == 0 and c < 2,
                                              part == 1 and c >= 2)
                            last.then_inc(s["o_full"] if part else s["o_half"], 1)
            pe.wait_ge(s["o_free"], rounds * NE + 1)
            scatter(1, s["y_full"])


def kernel(x, mem, g_mix, g_mem, w_in, b_merge, nsa_q_norm, nsa_k_norm, cmp_pe, cmp_w1, cmp_b1, cmp_w2,
           rwkv_shift_mix, rwkv_w0, rwkv_w_up, rwkv_a0, rwkv_a_up, rwkv_g_up, rwkv_k_k, rwkv_k_a, rwkv_r_k,
           rwkv_ln_w, rwkv_ln_b, mem_w_kv, mem_q_norm, mem_k_norm, w_branch, w_out, g_ffn,
           router_w, router_b, exp_w1, exp_b1, exp_w2, exp_b2):
    from concourse import bacc
    from concourse.bass_utils import run_bass_kernel_spmd

    def rows(w):
        w = np.asarray(w)
        return np.ascontiguousarray(w.reshape(-1, P, w.shape[-1]).transpose(1, 0, 2))

    w_in = np.asarray(w_in)[0]
    at, parts = 0, {}
    for name, n in (("q", 512), ("kcmp", 128), ("vcmp", 128), ("kslc", 128), ("vslc", 128), ("kwin", 128),
                    ("vwin", 128), ("gate", 24), ("shift", 1792), ("qm", 512), ("merge", 3072)):
        parts[name] = w_in[:, at:at + n]
        at += n
    kv = np.asarray(mem_w_kv)[0]
    blocks = [parts["shift"][:, n * 512:(n + 1) * 512] for n in range(4)]
    blocks += [parts["q"], np.concatenate([parts[n] for n in ("kslc", "kwin", "kcmp", "vcmp")], 1),
               np.concatenate([parts[n] for n in ("vslc", "vwin", "gate")], 1), parts["qm"], kv[:, :512], kv[:, 512:]]
    merge = [parts["merge"][:, n * 512:(n + 1) * 512] for n in range(6)]
    weights = np.zeros((len(W1_UNITS), P, UNIT), np.float32)

    def put(name, w):
        weights[W1_AT[name]].reshape(P, w.shape[1], -1)[:, :, :w.shape[2]] = w

    for name, w in zip(("shift0", "shift1", "shift2", "shift3", "q", "kc", "vg", "qm", "km", "vm"), blocks):
        put(name, rows(w))
    weights[W1_AT["cmp1"]] = np.asarray(cmp_w1)[0].reshape(2, 16, P, P).transpose(2, 0, 1, 3).reshape(P, UNIT)
    for n, w in enumerate(merge):
        put(f"merge{n}", rows(w))
    for n in range(3):
        put(f"branch{n}", rows(np.asarray(w_branch)[0, n]))
    for n in range(2):
        put(f"out{n}", rows(np.asarray(w_out)[0, n * 512:(n + 1) * 512]))

    vec = np.zeros((P, NVEC), np.float32)
    for name, a in (("g_mix", g_mix), ("g_mem", g_mem), ("g_ffn", g_ffn), ("b_merge", b_merge),
                    ("mix", rwkv_shift_mix), ("w0", rwkv_w0), ("a0", rwkv_a0), ("k_k", rwkv_k_k), ("k_a", rwkv_k_a),
                    ("r_k", rwkv_r_k), ("ln_w", rwkv_ln_w), ("ln_b", rwkv_ln_b), ("cmp_b1", cmp_b1),
                    ("mq_n", mem_q_norm), ("mk_n", mem_k_norm)):
        o, n = VEC[name]
        vec[:, o:o + n] = np.asarray(a).reshape(n, P).T

    w1 = np.asarray(exp_w1)[0].reshape(NE, KD, P, 4, 256, 2)
    experts = np.empty((NE, UNITS2, P, UNIT), np.float32)
    experts[:, 0:4].reshape(NE, 4, P, KD, 2, 256)[...] = w1.transpose(0, 3, 2, 1, 5, 4)
    experts[:, 4:6].reshape(NE, 2, P, 4, D)[...] = np.asarray(exp_w2)[0].reshape(NE, 2, 4, P, D).transpose(0, 1, 3, 2, 4)
    b1 = np.asarray(exp_b1)[0].reshape(NE, 4, 2, P, 2).transpose(3, 0, 1, 4, 2)
    q_n, k_n = np.asarray(nsa_q_norm)[0], np.asarray(nsa_k_norm)[0]
    arrays = {
        "x": np.asarray(x), "mem": np.asarray(mem), "weights": weights, "const": shape_constants(), "vec": vec,
        "experts": experts, "exp_b1": np.ascontiguousarray(b1).reshape(P, NE * 16),
        "exp_b2": np.asarray(exp_b2)[0],
        "up": np.concatenate([np.concatenate([np.asarray(rwkv_w_up)[0], np.asarray(rwkv_a_up)[0]], 0),
                              np.asarray(rwkv_g_up)[0]], 1),
        "cmp_w2": np.ascontiguousarray(np.asarray(cmp_w2)[0].transpose(1, 0, 2)).reshape(P, 2 * DH),
        "cmp_pe": np.ascontiguousarray(np.asarray(cmp_pe)[0].reshape(2, 16, P).transpose(2, 0, 1)).reshape(P, 32),
        "head_norms": np.concatenate([q_n] * 8 + [k_n[1]] * 2 + [k_n[2]] * 2)[None],
        "cmp_norm": k_n[0][None],
        "router_w": rows(np.asarray(router_w)[0]).reshape(P, KD * NE), "router_b": np.asarray(router_b),
    }
    nc = bacc.Bacc("TRN2", target_bir_lowering=False, num_devices=1)
    ins = {}
    for name, arr in arrays.items():
        arr = arrays[name] = np.ascontiguousarray(arr)
        ins[name] = nc.dram_tensor(name, arr.shape, F32, kind="ExternalInput").ap()
    out = nc.dram_tensor("out", (1, S, D), F32, kind="ExternalOutput").ap()
    build(nc, ins, out)
    r = run_bass_kernel_spmd(nc, [arrays], core_ids=[0])
    return r.results[0]["out"]
```
